# Optimizing a Trainium2 kernel written in Bass

```python
import jax
import jax.numpy as jnp
from jax import lax
import numpy as np
import math
import jax, jax.numpy as jnp

D_MODEL = 1024
BATCH = 1
SEQ = 256
DEPTH = 2

GRID_W = 64
MEM_LEN = 256
HEAD_DIM = 64
Q_BLOCK = 128
ROPE_THETA = 10000.0
LN_EPS = 1e-5
RMS_EPS = 1e-6
NA_HEADS = 4
NA_ROWS = 8
NA_COLS = 16
GQA_HEADS = 8
GQA_KV_HEADS = 2
GQA_GROUP = GQA_HEADS // GQA_KV_HEADS
MLA_HEADS = 4
MLA_Q_RANK = 256
MLA_KV_RANK = 128
MLA_NOPE = 64
MLA_ROPE = 32
MLA_V = 64
N_BRANCH = 3
A_WIDTH = NA_HEADS * HEAD_DIM
B_WIDTH = GQA_HEADS * HEAD_DIM
C_WIDTH = MLA_HEADS * MLA_V
IN_SPLITS = (A_WIDTH, A_WIDTH, A_WIDTH,
             B_WIDTH, GQA_KV_HEADS * HEAD_DIM, GQA_KV_HEADS * HEAD_DIM,
             MLA_Q_RANK, MLA_KV_RANK, MLA_ROPE,
             N_BRANCH * D_MODEL)
IN_COLS = sum(IN_SPLITS)
MEM_HEADS = 4
MEM_HEAD_DIM = D_MODEL // MEM_HEADS
D_FF = ((8 * D_MODEL // 3 + 127) // 128) * 128
N_EXPERTS = 8
TOP_K = 2
N_DENSE = (DEPTH + 1) // 2
N_MOE = DEPTH // 2
ALPHA = (2 * DEPTH) ** 0.25
BETA = (8 * DEPTH) ** -0.25


def layer_norm(x, g, b):
    xf = x.astype(jnp.float32)
    mu = jnp.mean(xf, axis=-1, keepdims=True)
    var = jnp.mean(jnp.square(xf - mu), axis=-1, keepdims=True)
    return ((xf - mu) * lax.rsqrt(var + LN_EPS) * g + b).astype(x.dtype)

def rms_norm(x, g):
    xf = x.astype(jnp.float32)
    return (xf * lax.rsqrt(jnp.mean(xf * xf, axis=-1, keepdims=True) + RMS_EPS) * g).astype(x.dtype)

def axial_rope_angles(seq, rot_dim):
    t = jnp.arange(seq)
    row = (t // GRID_W).astype(jnp.float32)
    col = (t % GRID_W).astype(jnp.float32)
    n = rot_dim // 4
    inv_freq = ROPE_THETA ** (-jnp.arange(n, dtype=jnp.float32) / n)
    ang = jnp.concatenate([row[:, None] * inv_freq, col[:, None] * inv_freq], axis=-1)
    return jnp.cos(ang), jnp.sin(ang)

def apply_rope(x, cos, sin):
    half = x.shape[-1] // 2
    xf = x.astype(jnp.float32)
    x1, x2 = xf[..., :half], xf[..., half:]
    c, s = cos[None, :, None, :], sin[None, :, None, :]
    return jnp.concatenate([x1 * c - x2 * s, x2 * c + x1 * s], axis=-1).astype(x.dtype)

def blocked_attention(q, k, v, scale):
    b, s, hkv, g, dk = q.shape
    nb = s // Q_BLOCK
    qb = q.reshape(b, nb, Q_BLOCK, hkv, g, dk).swapaxes(0, 1)

    def attend(q_blk):
        sc = jnp.einsum('bqhgd,bkhd->bhgqk', q_blk, k).astype(jnp.float32) * scale
        p = jax.nn.softmax(sc, axis=-1).astype(v.dtype)
        return jnp.einsum('bhgqk,bkhd->bqhgd', p, v)

    o = lax.map(attend, qb)
    return o.swapaxes(0, 1).reshape(b, s, hkv * g * v.shape[-1])

def neighborhood_attention(q, k, v, rpb):
    b, s, h, d = q.shape
    rows = s // GRID_W
    kr = min(NA_ROWS, rows)
    n_keys = kr * NA_COLS
    r = jnp.arange(rows)
    c = jnp.arange(GRID_W)
    key_r = jnp.clip(r - kr // 2, 0, rows - kr)[:, None] + jnp.arange(kr)
    key_c = jnp.clip(c - NA_COLS // 2, 0, GRID_W - NA_COLS)[:, None] + jnp.arange(NA_COLS)
    idx = (key_r[:, None, :, None] * GRID_W + key_c[None, :, None, :]).reshape(rows, GRID_W, n_keys)
    dr = key_r - r[:, None] + (NA_ROWS - 1)
    dc = key_c - c[:, None] + (NA_COLS - 1)
    bias = rpb[:, dr[:, None, :, None], dc[None, :, None, :]]
    bias = bias.reshape(h, rows, GRID_W, n_keys).transpose(1, 0, 2, 3)
    q_rows = q.reshape(b, rows, GRID_W, h, d).swapaxes(0, 1)
    scale = d ** -0.5

    def attend_row(args):
        q_r, idx_r, bias_r = args
        k_g = k[:, idx_r]
        v_g = v[:, idx_r]
        sc = jnp.einsum('bwhd,bwnhd->bhwn', q_r, k_g).astype(jnp.float32) * scale + bias_r.astype(jnp.float32)
        p = jax.nn.softmax(sc, axis=-1).astype(v.dtype)
        return jnp.einsum('bhwn,bwnhd->bwhd', p, v_g)

    o = lax.map(attend_row, (q_rows, idx, bias))
    return o.swapaxes(0, 1).reshape(b, s, h * d)

def hybrid_mixer(h, w_in, na_rpb, gqa_q_norm, gqa_k_norm, mla_q_norm, mla_kv_norm,
                 mla_w_uq, mla_w_ukv, w_proj_a, w_proj_b, w_proj_c, w_out, rope_b, rope_c):
    b, s, _ = h.shape
    z = h @ w_in
    (a_q, a_k, a_v, b_q, b_k, b_v, c_dq, c_dkv, c_kr, gate_logits) = jnp.split(
        z, np.cumsum(IN_SPLITS)[:-1].tolist(), axis=-1)

    ya = neighborhood_attention(a_q.reshape(b, s, NA_HEADS, HEAD_DIM),
                                a_k.reshape(b, s, NA_HEADS, HEAD_DIM),
                                a_v.reshape(b, s, NA_HEADS, HEAD_DIM), na_rpb)

    cos_b, sin_b = rope_b
    qb = apply_rope(rms_norm(b_q.reshape(b, s, GQA_HEADS, HEAD_DIM), gqa_q_norm), cos_b, sin_b)
    kb = apply_rope(rms_norm(b_k.reshape(b, s, GQA_KV_HEADS, HEAD_DIM), gqa_k_norm), cos_b, sin_b)
    vb = b_v.reshape(b, s, GQA_KV_HEADS, HEAD_DIM)
    yb = blocked_attention(qb.reshape(b, s, GQA_KV_HEADS, GQA_GROUP, HEAD_DIM), kb, vb, HEAD_DIM ** -0.5)

    cos_c, sin_c = rope_c
    qc = (rms_norm(c_dq, mla_q_norm) @ mla_w_uq).reshape(b, s, MLA_HEADS, MLA_NOPE + MLA_ROPE)
    q_nope, q_pe = qc[..., :MLA_NOPE], apply_rope(qc[..., MLA_NOPE:], cos_c, sin_c)
    kvc = (rms_norm(c_dkv, mla_kv_norm) @ mla_w_ukv).reshape(b, s, MLA_HEADS, MLA_NOPE + MLA_V)
    k_nope, vc = kvc[..., :MLA_NOPE], kvc[..., MLA_NOPE:]
    k_pe = apply_rope(c_kr[:, :, None, :], cos_c, sin_c)
    q_full = jnp.concatenate([q_nope, q_pe], axis=-1)[:, :, :, None, :]
    k_full = jnp.concatenate([k_nope, jnp.broadcast_to(k_pe, (b, s, MLA_HEADS, MLA_ROPE))], axis=-1)
    yc = blocked_attention(q_full, k_full, vc, (MLA_NOPE + MLA_ROPE) ** -0.5)

    gates = jax.nn.sigmoid(gate_logits.astype(jnp.float32)).astype(h.dtype).reshape(b, s, N_BRANCH, D_MODEL)
    merged = (gates[:, :, 0] * (ya @ w_proj_a)
              + gates[:, :, 1] * (yb @ w_proj_b)
              + gates[:, :, 2] * (yc @ w_proj_c))
    return merged @ w_out

def memory_cross_attention(h, mem, wq, wkv, wo):
    b, s, _ = h.shape
    m = mem.shape[1]
    q = (h @ wq).reshape(b, s, MEM_HEADS, MEM_HEAD_DIM)
    kv = (mem @ wkv).reshape(b, m, 2, MEM_HEADS, MEM_HEAD_DIM)
    k, v = kv[:, :, 0], kv[:, :, 1]
    sc = jnp.einsum('bqhd,bkhd->bhqk', q, k).astype(jnp.float32) * (MEM_HEAD_DIM ** -0.5)
    p = jax.nn.softmax(sc, axis=-1).astype(v.dtype)
    o = jnp.einsum('bhqk,bkhd->bqhd', p, v).reshape(b, s, D_MODEL)
    return o @ wo

def swiglu(t, w_gu, w_down):
    a, g = jnp.split(t @ w_gu, 2, axis=-1)
    return (jax.nn.silu(a) * g) @ w_down

def moe_swiglu(h, w_router, w_gu, w_down):
    b, s, d = h.shape
    t = h.reshape(b * s, d)
    logits = (t @ w_router).astype(jnp.float32)
    top_logit, top_idx = lax.top_k(logits, TOP_K)
    top_w = jax.nn.softmax(top_logit, axis=-1)
    gate = jnp.einsum('tk,tke->te', top_w,
                      jax.nn.one_hot(top_idx, N_EXPERTS, dtype=jnp.float32)).astype(h.dtype)
    out = jnp.zeros_like(t)
    for e in range(N_EXPERTS):
        out = out + gate[:, e:e + 1] * swiglu(t, w_gu[e], w_down[e])
    return out.reshape(b, s, d)

def first_inputs(seed: int = 0) -> dict:
    key = jax.random.key(seed)
    k = jax.random.split(key, 26)

    def nrm(kk, shape, std):
        return jax.random.normal(kk, shape, jnp.float32) * std

    def gain(kk, shape):
        return 1.0 + 0.05 * jax.random.normal(kk, shape, jnp.float32)

    return {
        'x': nrm(k[0], (BATCH, SEQ, D_MODEL), 1.0),
        'mem': nrm(k[1], (BATCH, MEM_LEN, D_MODEL), 1.0),
        'emb_ln_g': gain(k[2], (D_MODEL,)),
        'emb_ln_b': nrm(k[3], (D_MODEL,), 0.02),
        'w_in': nrm(k[4], (DEPTH, D_MODEL, IN_COLS), D_MODEL ** -0.5),
        'na_rpb': nrm(k[5], (DEPTH, NA_HEADS, 2 * NA_ROWS - 1, 2 * NA_COLS - 1), 0.1),
        'gqa_q_norm': gain(k[6], (DEPTH, HEAD_DIM)),
        'gqa_k_norm': gain(k[7], (DEPTH, HEAD_DIM)),
        'mla_q_norm': gain(k[8], (DEPTH, MLA_Q_RANK)),
        'mla_kv_norm': gain(k[9], (DEPTH, MLA_KV_RANK)),
        'mla_w_uq': nrm(k[10], (DEPTH, MLA_Q_RANK, MLA_HEADS * (MLA_NOPE + MLA_ROPE)), MLA_Q_RANK ** -0.5),
        'mla_w_ukv': nrm(k[11], (DEPTH, MLA_KV_RANK, MLA_HEADS * (MLA_NOPE + MLA_V)), MLA_KV_RANK ** -0.5),
        'w_proj_a': nrm(k[12], (DEPTH, A_WIDTH, D_MODEL), A_WIDTH ** -0.5),
        'w_proj_b': nrm(k[13], (DEPTH, B_WIDTH, D_MODEL), B_WIDTH ** -0.5),
        'w_proj_c': nrm(k[14], (DEPTH, C_WIDTH, D_MODEL), C_WIDTH ** -0.5),
        'w_out': nrm(k[15], (DEPTH, D_MODEL, D_MODEL), BETA * D_MODEL ** -0.5),
        'mem_wq': nrm(k[16], (DEPTH, D_MODEL, D_MODEL), D_MODEL ** -0.5),
        'mem_wkv': nrm(k[17], (DEPTH, D_MODEL, 2 * D_MODEL), D_MODEL ** -0.5),
        'mem_wo': nrm(k[18], (DEPTH, D_MODEL, D_MODEL), BETA * D_MODEL ** -0.5),
        'ln_g': gain(k[19], (DEPTH, 3, D_MODEL)),
        'ln_b': nrm(k[20], (DEPTH, 3, D_MODEL), 0.02),
        'ffn_w_gu': nrm(k[21], (N_DENSE, D_MODEL, 2 * D_FF), D_MODEL ** -0.5),
        'ffn_w_down': nrm(k[22], (N_DENSE, D_FF, D_MODEL), BETA * D_FF ** -0.5),
        'moe_router': nrm(k[23], (N_MOE, D_MODEL, N_EXPERTS), D_MODEL ** -0.5),
        'moe_w_gu': nrm(k[24], (N_MOE, N_EXPERTS, D_MODEL, 2 * D_FF), D_MODEL ** -0.5),
        'moe_w_down': nrm(k[25], (N_MOE, N_EXPERTS, D_FF, D_MODEL), BETA * D_FF ** -0.5),
    }

def first_block(x, mem, emb_ln_g, emb_ln_b, w_in, na_rpb, gqa_q_norm, gqa_k_norm, mla_q_norm,
              mla_kv_norm, mla_w_uq, mla_w_ukv, w_proj_a, w_proj_b, w_proj_c, w_out,
              mem_wq, mem_wkv, mem_wo, ln_g, ln_b, ffn_w_gu, ffn_w_down,
              moe_router, moe_w_gu, moe_w_down):
    s = x.shape[1]
    rope_b = axial_rope_angles(s, HEAD_DIM)
    rope_c = axial_rope_angles(s, MLA_ROPE)
    h = layer_norm(x, emb_ln_g, emb_ln_b)
    for l in range(DEPTH):
        mix = hybrid_mixer(h, w_in[l], na_rpb[l], gqa_q_norm[l], gqa_k_norm[l], mla_q_norm[l],
                           mla_kv_norm[l], mla_w_uq[l], mla_w_ukv[l], w_proj_a[l], w_proj_b[l],
                           w_proj_c[l], w_out[l], rope_b, rope_c)
        h = layer_norm(ALPHA * h + mix, ln_g[l, 0], ln_b[l, 0])
        xa = memory_cross_attention(h, mem, mem_wq[l], mem_wkv[l], mem_wo[l])
        h = layer_norm(ALPHA * h + xa, ln_g[l, 1], ln_b[l, 1])
        if l % 2 == 0:
            f = swiglu(h, ffn_w_gu[l // 2], ffn_w_down[l // 2])
        else:
            f = moe_swiglu(h, moe_router[l // 2], moe_w_gu[l // 2], moe_w_down[l // 2])
        h = layer_norm(ALPHA * h + f, ln_g[l, 2], ln_b[l, 2])
    return h


ATT_HEADS = D_MODEL // HEAD_DIM
ATT_WIDTH = ATT_HEADS * HEAD_DIM
ROT_DIM = HEAD_DIM // 4
ROPE_THETA_2 = 500000.0
DILATED_PATTERNS = ((128, 1), (512, 4), (2048, 16))
MAX_REACH = 2048
SSM_WIDTH = D_MODEL // 2
SSM_GROUP = 16
SSM_GROUPS = SSM_WIDTH // SSM_GROUP
SSM_STATE = 64
POOL_WIDTH = 2 * D_MODEL
POOL_WINDOWS = (2, 4, 8, 16)
POOL_GROUP = POOL_WIDTH // len(POOL_WINDOWS)
EVEN_IN = 4 * ATT_WIDTH + 2 * SSM_WIDTH
EVEN_OUT = ATT_WIDTH + SSM_WIDTH
ODD_IN = 2 * POOL_WIDTH
N_EVEN = (DEPTH + 1) // 2
N_ODD = DEPTH // 2


def rmsnorm(x, gain):
    xf = x.astype(jnp.float32)
    y = xf * lax.rsqrt(jnp.mean(xf * xf, axis=-1, keepdims=True) + RMS_EPS)
    return (y * gain.astype(jnp.float32)).astype(x.dtype)

def apply_partial_rope(x, pos):
    half = ROT_DIM // 2
    inv_freq = ROPE_THETA_2 ** (-jnp.arange(0, ROT_DIM, 2, dtype=jnp.float32) / ROT_DIM)
    ang = pos.astype(jnp.float32)[:, None] * inv_freq[None, :]
    cos = jnp.cos(ang)[None, :, None, :]
    sin = jnp.sin(ang)[None, :, None, :]
    xr = x[..., :ROT_DIM].astype(jnp.float32)
    x1, x2 = xr[..., :half], xr[..., half:]
    rot = jnp.concatenate([x1 * cos - x2 * sin, x2 * cos + x1 * sin], axis=-1)
    return jnp.concatenate([rot.astype(x.dtype), x[..., ROT_DIM:]], axis=-1)

def dilated_offsets():
    return np.concatenate([np.arange(w // d + 1) * d for w, d in DILATED_PATTERNS]).astype(np.int32)

def dilated_attention(q, k, v):
    b, s, h, dh = q.shape
    offsets = jnp.asarray(dilated_offsets())
    qh = q.transpose(0, 2, 1, 3)
    pad = ((0, 0), (0, 0), (MAX_REACH, 0), (0, 0))
    k_pad = jnp.pad(k.transpose(0, 2, 1, 3), pad)
    v_pad = jnp.pad(v.transpose(0, 2, 1, 3), pad)

    def block(bi):
        start = bi * Q_BLOCK
        q_blk = lax.dynamic_slice_in_dim(qh, start, Q_BLOCK, axis=2)
        rel = start + jnp.arange(Q_BLOCK, dtype=jnp.int32)[:, None] - offsets[None, :]
        k_g = k_pad[:, :, rel + MAX_REACH]
        v_g = v_pad[:, :, rel + MAX_REACH]
        scores = jnp.einsum('bhqd,bhqkd->bhqk', q_blk, k_g).astype(jnp.float32)
        scores = jnp.where(rel >= 0, scores, -jnp.inf)
        p = jax.nn.softmax(scores, axis=-1)
        return jnp.einsum('bhqk,bhqkd->bhqd', p.astype(v.dtype), v_g)

    out = lax.map(block, jnp.arange(s // Q_BLOCK, dtype=jnp.int32))
    return out.transpose(1, 0, 3, 2, 4).reshape(b, s, h * dh)

def s5_ssm(u, a_re, a_im, log_dt, b_re, b_im, c_re, c_im, d_skip, glu_w, glu_b):
    bsz, s, _ = u.shape
    f32 = jnp.float32
    uf = u.astype(f32)
    ug = uf.reshape(bsz, s, SSM_GROUPS, SSM_GROUP)
    lam = lax.complex(a_re.astype(f32), a_im.astype(f32))
    dt = jnp.exp(log_dt.astype(f32))[:, None]
    lam_bar = jnp.exp(lam * dt)
    b_mat = lax.complex(b_re.astype(f32), b_im.astype(f32))
    b_bar = ((lam_bar - 1.0) / lam)[..., None] * b_mat
    bu = jnp.einsum('bsgh,gph->bsgp', ug.astype(jnp.complex64), b_bar)
    a_seq = jnp.broadcast_to(lam_bar, bu.shape)

    def combine(left, right):
        a_l, s_l = left
        a_r, s_r = right
        return a_r * a_l, a_r * s_l + s_r

    _, states = lax.associative_scan(combine, (a_seq, bu), axis=1)
    c_mat = lax.complex(c_re.astype(f32), c_im.astype(f32))
    y = jnp.real(jnp.einsum('bsgp,ghp->bsgh', states, c_mat)).reshape(bsz, s, SSM_WIDTH)
    y = jax.nn.gelu(y + d_skip.astype(f32) * uf)
    y = y * jax.nn.sigmoid(y @ glu_w.astype(f32) + glu_b.astype(f32))
    return y.astype(u.dtype)

def multiscale_pool(u, pool_w, pool_scale):
    bsz, s, _ = u.shape
    ug = u.astype(jnp.float32).reshape(bsz, s, len(POOL_WINDOWS), POOL_GROUP)
    count_base = jnp.arange(1, s + 1, dtype=jnp.float32)[None, :, None]
    outs = []
    for g, w in enumerate(POOL_WINDOWS):
        ch = ug[:, :, g]
        cs = jnp.cumsum(ch, axis=1)
        lagged = jnp.pad(cs, ((0, 0), (w, 0), (0, 0)))[:, :s]
        mean = (cs - lagged) / jnp.minimum(count_base, float(w))
        outs.append(mean - ch)
    mixed = jnp.stack(outs, axis=2)
    y = jnp.einsum('bsgc,gcd->bsgd', mixed, pool_w.astype(jnp.float32)).reshape(bsz, s, POOL_WIDTH)
    return (y * pool_scale.astype(jnp.float32)).astype(u.dtype)

def even_mixer(h, w_in, w_out, a_re, a_im, log_dt, b_re, b_im, c_re, c_im, d_skip, glu_w, glu_b):
    bsz, s, _ = h.shape
    proj = h @ w_in
    cuts = [ATT_WIDTH, 2 * ATT_WIDTH, 3 * ATT_WIDTH, 4 * ATT_WIDTH, 4 * ATT_WIDTH + SSM_WIDTH]
    q, k, v, g_att, u_ssm, g_ssm = jnp.split(proj, cuts, axis=-1)
    pos = jnp.arange(s, dtype=jnp.int32)
    q = apply_partial_rope(q.reshape(bsz, s, ATT_HEADS, HEAD_DIM), pos) * (HEAD_DIM ** -0.5)
    k = apply_partial_rope(k.reshape(bsz, s, ATT_HEADS, HEAD_DIM), pos)
    v = v.reshape(bsz, s, ATT_HEADS, HEAD_DIM)
    att = dilated_attention(q, k, v)
    ssm = s5_ssm(u_ssm, a_re, a_im, log_dt, b_re, b_im, c_re, c_im, d_skip, glu_w, glu_b)
    merged = jnp.concatenate([att * jax.nn.silu(g_att), ssm * jax.nn.silu(g_ssm)], axis=-1)
    return merged @ w_out

def odd_mixer(h, w_in, pool_w, pool_scale, w_out):
    u, gate = jnp.split(h @ w_in, [POOL_WIDTH], axis=-1)
    y = multiscale_pool(u, pool_w, pool_scale)
    return (y * jax.nn.silu(gate)) @ w_out

def second_inputs(seed: int = 0) -> dict:
    key = jax.random.key(seed)
    ks = jax.random.split(key, 24)
    f32 = jnp.float32

    def nrm(k, shape, scale):
        return jax.random.normal(k, shape, f32) * scale

    n_idx = jnp.arange(SSM_STATE, dtype=f32)
    return {
        "x": jax.random.normal(ks[0], (BATCH, SEQ, D_MODEL), f32),
        "pre_norm": 1.0 + nrm(ks[1], (DEPTH, D_MODEL), 0.1),
        "post_norm": 1.0 + nrm(ks[2], (DEPTH, D_MODEL), 0.1),
        "even_w_in": nrm(ks[3], (N_EVEN, D_MODEL, EVEN_IN), D_MODEL ** -0.5),
        "even_w_out": nrm(ks[4], (N_EVEN, EVEN_OUT, D_MODEL), EVEN_OUT ** -0.5),
        "ssm_a_re": -0.5 + nrm(ks[5], (N_EVEN, SSM_GROUPS, SSM_STATE), 0.01),
        "ssm_a_im": math.pi * n_idx + nrm(ks[6], (N_EVEN, SSM_GROUPS, SSM_STATE), 0.01),
        "ssm_log_dt": jax.random.uniform(ks[7], (N_EVEN, SSM_GROUPS), f32, math.log(1e-3), math.log(1e-1)),
        "ssm_b_re": nrm(ks[8], (N_EVEN, SSM_GROUPS, SSM_STATE, SSM_GROUP), (2 * SSM_GROUP) ** -0.5),
        "ssm_b_im": nrm(ks[9], (N_EVEN, SSM_GROUPS, SSM_STATE, SSM_GROUP), (2 * SSM_GROUP) ** -0.5),
        "ssm_c_re": nrm(ks[10], (N_EVEN, SSM_GROUPS, SSM_GROUP, SSM_STATE), (2 * SSM_STATE) ** -0.5),
        "ssm_c_im": nrm(ks[11], (N_EVEN, SSM_GROUPS, SSM_GROUP, SSM_STATE), (2 * SSM_STATE) ** -0.5),
        "ssm_d": nrm(ks[12], (N_EVEN, SSM_WIDTH), 1.0),
        "ssm_glu_w": nrm(ks[13], (N_EVEN, SSM_WIDTH, SSM_WIDTH), SSM_WIDTH ** -0.5),
        "ssm_glu_b": nrm(ks[14], (N_EVEN, SSM_WIDTH), 0.02),
        "odd_w_in": nrm(ks[15], (N_ODD, D_MODEL, ODD_IN), D_MODEL ** -0.5),
        "pool_w": nrm(ks[16], (N_ODD, len(POOL_WINDOWS), POOL_GROUP, POOL_GROUP), POOL_GROUP ** -0.5),
        "pool_scale": 1.0 + nrm(ks[17], (N_ODD, POOL_WIDTH), 0.1),
        "odd_w_out": nrm(ks[18], (N_ODD, POOL_WIDTH, D_MODEL), POOL_WIDTH ** -0.5),
    }

def second_block(x, pre_norm, post_norm, even_w_in, even_w_out, ssm_a_re, ssm_a_im, ssm_log_dt,
              ssm_b_re, ssm_b_im, ssm_c_re, ssm_c_im, ssm_d, ssm_glu_w, ssm_glu_b,
              odd_w_in, pool_w, pool_scale, odd_w_out):
    for layer in range(DEPTH):
        h = rmsnorm(x, pre_norm[layer])
        i = layer // 2
        if layer % 2 == 0:
            y = even_mixer(h, even_w_in[i], even_w_out[i], ssm_a_re[i], ssm_a_im[i], ssm_log_dt[i],
                           ssm_b_re[i], ssm_b_im[i], ssm_c_re[i], ssm_c_im[i], ssm_d[i],
                           ssm_glu_w[i], ssm_glu_b[i])
        else:
            y = odd_mixer(h, odd_w_in[i], pool_w[i], pool_scale[i], odd_w_out[i])
        x = x + rmsnorm(y, post_norm[layer])
    return x


def setup_inputs(seed=0):
    out = dict(first_inputs(seed))
    for name, value in second_inputs(seed + 1).items():
        if name != "x":
            out[name + "_2"] = value
    return out


def reference(
    x, mem, emb_ln_g, emb_ln_b, w_in, na_rpb, gqa_q_norm, gqa_k_norm, mla_q_norm, mla_kv_norm,
    mla_w_uq, mla_w_ukv, w_proj_a, w_proj_b, w_proj_c, w_out, mem_wq, mem_wkv, mem_wo, ln_g,
    ln_b, ffn_w_gu, ffn_w_down, moe_router, moe_w_gu, moe_w_down, pre_norm_2, post_norm_2,
    even_w_in_2, even_w_out_2, ssm_a_re_2, ssm_a_im_2, ssm_log_dt_2, ssm_b_re_2, ssm_b_im_2,
    ssm_c_re_2, ssm_c_im_2, ssm_d_2, ssm_glu_w_2, ssm_glu_b_2, odd_w_in_2, pool_w_2,
    pool_scale_2, odd_w_out_2,
):
    x = first_block(
        x, mem, emb_ln_g, emb_ln_b, w_in, na_rpb, gqa_q_norm, gqa_k_norm, mla_q_norm,
        mla_kv_norm, mla_w_uq, mla_w_ukv, w_proj_a, w_proj_b, w_proj_c, w_out, mem_wq, mem_wkv,
        mem_wo, ln_g, ln_b, ffn_w_gu, ffn_w_down, moe_router, moe_w_gu, moe_w_down,
    )
    return second_block(
        x, pre_norm_2, post_norm_2, even_w_in_2, even_w_out_2, ssm_a_re_2, ssm_a_im_2,
        ssm_log_dt_2, ssm_b_re_2, ssm_b_im_2, ssm_c_re_2, ssm_c_im_2, ssm_d_2, ssm_glu_w_2,
        ssm_glu_b_2, odd_w_in_2, pool_w_2, pool_scale_2, odd_w_out_2,
    )


_drawn_inputs = setup_inputs


def setup_inputs(seed=0):
    import zlib

    import numpy as np

    out = dict(_drawn_inputs(seed))
    spreads = {}
    factors = {'na_rpb': 2.83,
     'gqa_q_norm': 8.0,
     'gqa_k_norm': 8.0,
     'mla_q_norm': 4.377,
     'mla_kv_norm': 3.814,
     'ssm_a_re_2': 200.0,
     'ssm_glu_b_2': 8.0,
     'ssm_a_im_2': 30.76,
     'ssm_log_dt_2': 34.648,
     'ssm_b_re_2': 42.792,
     'ssm_b_im_2': 42.856,
     'ssm_c_re_2': 43.44,
     'ssm_c_im_2': 42.568}
    for name, (base, spread) in spreads.items():
        noise = np.random.default_rng([zlib.crc32(name.encode()), seed]).standard_normal(out[name].shape)
        drawn = base * np.exp(spread * noise) if base else spread * noise
        out[name] = jnp.asarray(drawn.astype(out[name].dtype))
    for name, factor in factors.items():
        out[name] = (out[name] * factor).astype(out[name].dtype)
    return out
```

```python
from contextlib import ExitStack, contextmanager

import numpy as np

import concourse.bass as bass
from concourse import mybir

ALU = mybir.AluOpType
ACT = mybir.ActivationFunctionType
F32 = mybir.dt.float32
U32 = mybir.dt.uint32
AX = mybir.AxisListType

P = 128
T = 256
NT = T // P
D = 1024
KD = D // P
DEPTH = 2
GRID_W = 64
HD = 64
ROPE_THETA = 10000.0
LN_EPS = 1e-5
RMS_EPS = 1e-6
NA_HEADS, NA_COLS = 4, 16
GQA_HEADS, GQA_KV = 8, 2
MLA_HEADS, NOPE, ROPE_C, MLA_V = 4, 64, 32, 64
DQ, DKV = 256, 128
MEM_HEADS, MEM_HD = 4, 256
D_FF = ((8 * D // 3 + 127) // 128) * 128
KF = D_FF // P
N_EXPERTS = 8
ALPHA = (2 * DEPTH) ** 0.25
A_Q, A_K, A_V = 0, 256, 512
B_Q, B_K, B_V = 768, 1280, 1408
C_DQ, C_DKV, C_KR = 1536, 1792, 1920
ZQ = 1952
ZIN = ZQ + 3 * D
Z_WIDTHS = [512, 512, 512, 416] + [512] * 6
ATT_HEADS = 16
ROT = 16
THETA_2 = 500000.0
SSM_W = 512
SSM_TILES = 16
E_Q, E_K, E_V, E_G, E_U, E_GS = 0, 1024, 2048, 3072, 4096, 4608
EVEN_IN, EVEN_OUT = 5120, 1536
POOL_W = 2048
POOL_WINDOWS = (2, 4, 8, 16)
NEG = -1.0e30
TWO_PI_HI = 6.28125
TWO_PI_LO = 2 * np.pi - TWO_PI_HI
TURN = 6.2831845
ROUND = 1.5 * 2.0 ** 23
TWO_PI = 2 * np.pi

SLOT = 5120
NSLOT = 4
HID_CHUNKS = D_FF // 256
DOWN_GROUPS = [5, 5, 4, 4, 4]
C_ID, C_COSB, C_SINB, C_COSC, C_SINC, C_COS2, C_SIN2, C_DMASK, C_DMUL = 0, 128, 192, 256, 288, 320, 336, 352, 864
C_TIME, C_IOTA8 = 1376, 1632
C_END = 1640


TILE_AT = [(m // 2) % 4 + 4 * (2 * (m // 8) + m % 2) for m in range(SSM_TILES)]


def weight_tiles(k_tiles, widths, group):
    off, out = 0, []
    for c, w in enumerate(widths):
        k = 0
        while k < k_tiles:
            n = min(group, k_tiles - k)
            out.append((c, k, n, w, off))
            off += n * w
            k += n
    return out


class Line:

    def __init__(self, eng, sems):
        self.eng, self.sems = eng, sems
        self.seen, self.reg, self.per = {}, None, {}

    def value(self, name, count):
        if self.reg is not None and self.per.get(name):
            return self.reg * self.per[name] + count
        return count

    def at(self, name, count):
        return self.sems(name), self.value(name, count)

    def next(self, name, k=1):
        self.seen[name] = self.seen.get(name, 0) + k
        return self.at(name, self.seen[name])

    def passed(self, name, k=1):
        self.seen[name] = self.seen.get(name, 0) + k

    @contextmanager
    def loop(self, n, per):
        before = dict(self.seen)
        self.per = per
        with self.eng.Fori(0, n) as reg:
            self.reg = reg
            yield reg
            self.reg = None
        for k, v in self.seen.items():
            d = v - before.get(k, 0)
            if d:
                assert per.get(k, 0) == d, (k, d, per.get(k))
                self.seen[k] += (n - 1) * d


class Banks:

    def __init__(self, name, n, views):
        self.name, self.n, self.views = name, n, views
        self.next, self.uses = 0, [0] * n

    def emptied(self, b):
        return f"{self.name}{b}_emptied"


def program(nc, d, out, stop=None):
    ctx = ExitStack()
    with ctx:
        def sb(name, shape, dt=F32):
            return ctx.enter_context(nc.sbuf_tensor(name, shape, dt))

        sem_table = {}

        def sems(name):
            if name not in sem_table:
                sem_table[name] = ctx.enter_context(nc.semaphore(name))
            return sem_table[name]

        weights = sb("weights", [P, NSLOT, SLOT])
        h = sb("h", [P, NT, D])
        hT = sb("hT", [P, KD, T])
        big_flat = sb("big", [P, NT * EVEN_IN])
        att = sb("att", [P, 6144])
        prob = sb("prob", [P, 2, NT, T])
        probT = sb("probT", [P, 2, NT, T])
        bias = sb("bias", [P, 2, NT, T])
        norm_par = sb("norm_par", [P, 2, 2, D])
        head_gain = sb("head_gain", [P, 1024])
        const = sb("const", [P, C_END])
        k_rope = sb("k_rope", [P, NT, ROPE_C])
        stats = sb("stats", [P, NT, 2, 6])
        mv = sb("mv", [P, NT, 2])
        rstd = sb("rstd", [P, NT, 16])
        smax = sb("smax", [P, 2, NT])
        rsum = sb("rsum", [P, 2, NT])
        ssum = sb("ssum", [P, 2, NT])
        router_w = sb("router_w", [P, KD, N_EXPERTS])
        logit = sb("logit", [P, NT, N_EXPERTS])
        top = sb("top", [P, NT, 8])
        top_i = sb("top_i", [P, NT, 8], U32)
        top_f = sb("top_f", [P, NT, 8])
        gate = sb("gate", [P, NT, N_EXPERTS + 1])
        tmp8 = sb("tmp8", [P, NT, N_EXPERTS])
        ssm_par = sb("ssm_par", [P, 3, SSM_TILES])
        ssm_s = sb("ssm_s", [P, 16, SSM_TILES])

        headT = att[:, 0:4096]
        yT = att[:, 4096:6144].rearrange("p (k t) -> p k t", t=T)
        big = big_flat[:, 0:NT * ZIN].rearrange("p (t n) -> p t n", t=NT)
        wide = big_flat[:, :].rearrange("p (t n) -> p t n", t=NT)
        ident = const[:, C_ID:C_ID + P]

        hidT = big_flat[:, 0:KF * T].rearrange("p (k t) -> p k t", t=T)
        hid = big_flat[:, KF * T:KF * T + 1024].rearrange("p (b t n) -> p b t n", b=2, t=NT)
        silu = att[:, 0:1024].rearrange("p (b t n) -> p b t n", b=2, t=NT)
        hv = headT.rearrange("p (n t) -> p n t", t=T)
        mergedA = att[:, 0:2048].rearrange("p (t n) -> p t n", t=NT)
        ssm_b = att[:, 2048:3072].rearrange("p (c j n) -> p c j n", c=2, j=4)
        ssm_c = att[:, 3072:4096].rearrange("p (c j n) -> p c j n", c=2, j=SSM_TILES)
        ssm_vec = att[:, 4096:5120].rearrange("p (c n) -> p c n", c=2)
        sinT = big_flat[:, 0:1024].rearrange("p (b i t) -> p b i t", b=2, i=2)
        cosT = big_flat[:, 1024:2048].rearrange("p (b i t) -> p b i t", b=2, i=2)
        rot_in = big_flat[:, 2048:3072].rearrange("p (c i t) -> p c i t", c=2, i=2)
        at1 = EVEN_IN
        tmpA = big_flat[:, at1:at1 + 512].rearrange("p (i t) -> p i t", i=2)
        tmpB = big_flat[:, at1 + 512:at1 + 1024].rearrange("p (i t) -> p i t", i=2)
        scanned = big_flat[:, at1 + 1024:at1 + 2048].rearrange("p (c i t) -> p c i t", c=2, i=2)
        ssm_state = big_flat[:, at1 + 2048:at1 + 3072].rearrange("p (c i t) -> p c i t", c=2, i=2)
        window = att[:, 4096:6144].rearrange("p (g s t) -> p g s t", g=4, s=NT)
        pool_scale = big_flat[:, 8192:10240]
        y_out = big_flat[:, 0:2048].rearrange("p (t n) -> p t n", t=NT)

        def e(t, col, n):
            return wide[:, t, col:col + n]

        def table(col, n):
            return const[:, col:col + NT * n].rearrange("p (t n) -> p t n", t=NT)

        pair_mem = [ctx.enter_context(nc.psum_tensor(f"pair{i}", [P, NT, 512], F32)) for i in range(2)]
        bank_mem = [ctx.enter_context(nc.psum_tensor(f"bank{i}", [P, 512], F32)) for i in range(4)]
        pairs = Banks("pair", 2, pair_mem)
        banks = Banks("bank", 4, bank_mem)
        jobs, tiles_used = {}, [0]

        block = ctx.enter_context(nc.Block())
        STAGES = ["emb", "mix0", "mem0", "ffn0", "mix1", "mem1", "ffn1", "even", "odd"]
        n_stages = len(STAGES) if stop is None else STAGES.index(stop) + 1

        def on(stage):
            return STAGES.index(stage) < n_stages

        PER_EXPERT = {"banks_filled": HID_CHUNKS * 2 + 2, "pair0_emptied": 7, "pair1_emptied": 6,
                      "bank0_emptied": 3, "bank1_emptied": 3, "bank2_emptied": 3, "bank3_emptied": 2,
                      "silu_done": HID_CHUNKS}
        for s in range(NSLOT):
            PER_EXPERT[f"slot{s}_landed"] = 16 * 4
            PER_EXPERT[f"slot{s}_used"] = 4

        @block.tensor
        def _(pe):
            L = Line(pe, sems)
            filled = [0]
            slot_owed = [None]

            def mm(o, lhsT, rhs, **flags):
                ins = pe.matmul(o, lhsT, rhs, **flags)
                if slot_owed[0] is not None:
                    ins.then_inc(sems(slot_owed[0]), 1)
                    slot_owed[0] = None
                return ins

            def mm_t(o, src, identity):
                return mm(o, src, identity, is_transpose=True, start=True, stop=True)

            def begin(ring, name, late=False):
                b = ring.next % ring.n
                ring.next += 1
                if ring.uses[b]:
                    pe.wait_ge(*L.at(ring.emptied(b), ring.uses[b]))
                ring.uses[b] += 1
                if not late:
                    filled[0] += 1
                jobs[name] = (ring, b, filled[0], ring.uses[b])
                return ring.views[b]

            def end_late(ins, name):
                ring, b, _, use = jobs[name]
                filled[0] += 1
                jobs[name] = (ring, b, filled[0], use)
                end(ins)

            def end(ins):
                ins.then_inc(sems("banks_filled"), 1)

            def emptied(name):
                ring, b, _, use = jobs[name]
                return L.at(ring.emptied(b), use)

            def transpose_rows(name, src, k_tiles):
                for j in range(0, k_tiles, 2):
                    o = begin(banks, (name, j))
                    n = min(2, k_tiles - j)
                    for i in range(n):
                        for t in range(NT):
                            ins = mm_t(o[:, (i * NT + t) * P:(i * NT + t + 1) * P], src(t, j + i), ident)
                    end(ins)

            def next_tile():
                n = tiles_used[0]
                tiles_used[0] += 1
                s = n % NSLOT
                pe.wait_ge(*L.at(f"slot{s}_landed", 16 * (n // NSLOT + 1)))
                return s

            def product(name, lhsT, k_tiles, widths, group):
                tiles = weight_tiles(k_tiles, widths, group)
                outs = []
                for c, k0, nk, w, _ in tiles:
                    s = next_tile()
                    n_out = -(-w // 512)
                    if k0 == 0:
                        outs = [begin(pairs, (name, c * n_out + i)) for i in range(n_out)]
                    for i, o in enumerate(outs):
                        n = min(512, w - 512 * i)
                        for t in range(NT):
                            for k in range(nk):
                                at = k * w + 512 * i
                                ins = mm(o[:, t, 0:n], lhsT(k0 + k, t), weights[:, s, at:at + n],
                                                start=(k0 + k == 0), stop=(k0 + k == k_tiles - 1))
                        if k0 + nk == k_tiles:
                            end(ins)
                    if k0 + nk == k_tiles:
                        slot_owed[0] = f"slot{s}_used"
                    else:
                        ins.then_inc(sems(f"slot{s}_used"), 1)

            def tiles_used_at(s):
                return (tiles_used[0] - 1) // NSLOT + 1

            def hT_at(k, t):
                return hT[:, k, t * P:(t + 1) * P]

            def yT_at(k, t):
                return yT[:, k, t * P:(t + 1) * P]

            def heads(name, specs):
                n = len(specs)
                for i in range(n + 2):
                    if i < n:
                        qk, v, width, natural = specs[i]
                        o = begin(banks, (name, "score", i))
                        for t in range(NT):
                            for j, (q, k) in enumerate(qk):
                                ins = mm(o[:, t * T:(t + 1) * T], q[:, t * P:(t + 1) * P], k,
                                                start=(j == 0), stop=(j == len(qk) - 1))
                        end(ins)
                    if 1 <= i <= n:
                        m = i - 1
                        pe.wait_ge(*L.next("prob_ready"))
                        o = begin(banks, (name, "probT", m))
                        for j in range(NT):
                            for t in range(NT):
                                at = (j * NT + t) * P
                                ins = mm_t(o[:, at:at + P], prob[:, m % 2, t, j * P:(j + 1) * P], ident)
                        end(ins)
                    if i >= 2:
                        m = i - 2
                        qk, v, width, natural = specs[m]
                        pe.wait_ge(*emptied((name, "probT", m)))
                        o = begin(banks, (name, "value", m))
                        if natural:
                            for t in range(NT):
                                for j in range(NT):
                                    ins = mm(o[:, t * width:(t + 1) * width],
                                                    probT[:, m % 2, j, t * P:(t + 1) * P], v(j),
                                                    start=(j == 0), stop=(j == NT - 1))
                        else:
                            for c in range(-(-width // P)):
                                w = min(P, width - c * P)
                                for j in range(NT):
                                    ins = mm(o[0:w, c * T:(c + 1) * T], v(j)[:, c * P:c * P + w],
                                                    probT[:, m % 2, j, :], start=(j == 0), stop=(j == NT - 1))
                        end(ins)

            def head_transposes(name, srcs):
                for j in range(0, len(srcs), 2):
                    o = begin(banks, (name, j))
                    for i, src in enumerate(srcs[j:j + 2]):
                        for t in range(NT):
                            ap = src(t)
                            w = ap.shape[1]
                            at = (i * NT + t) * P
                            ins = mm_t(o[0:w, at:at + P], ap, ident)
                    end(ins)

            def hd(base, n, w=HD):
                return [lambda t, i=i: big[:, t, base + i * w:base + (i + 1) * w] for i in range(n)]

            pe.wait_ge(*L.next("const_landed", 16))

            def mixer(l):
                pe.wait_ge(*L.next("normed"))
                transpose_rows(("hT", "mix", l), lambda t, k: h[:, t, k * P:(k + 1) * P], KD)
                pe.wait_ge(*emptied((("hT", "mix", l), KD - 2)))
                product(("z", l), hT_at, KD, Z_WIDTHS, KD)
                pe.wait_ge(*emptied((("z", l), 0)))
                pe.wait_ge(*emptied((("z", l), 1)))
                head_transposes(("aT", l), hd(A_Q, 4) + hd(A_K, 4))
                pe.wait_ge(*emptied((("aT", l), 4)))
                pe.wait_ge(*emptied((("aT", l), 6)))
                heads(("a", l), [([(hv[0:HD, i, :], hv[0:HD, 4 + i, :])],
                                  lambda j, i=i: big[:, j, A_V + i * HD:A_V + (i + 1) * HD], HD, False)
                                 for i in range(NA_HEADS)])
                pe.wait_ge(*L.next("b_rotated", 2))
                head_transposes(("bT", l), hd(B_Q, 10))
                pe.wait_ge(*emptied((("bT", l), 6)))
                pe.wait_ge(*emptied((("bT", l), 8)))
                heads(("b", l), [([(hv[0:HD, i, :], hv[0:HD, 8 + i // 4, :])],
                                  lambda j, i=i: big[:, j, B_V + i // 4 * HD:B_V + (i // 4 + 1) * HD], HD, False)
                                 for i in range(GQA_HEADS)])
                pe.wait_ge(*L.next("c_normed"))
                transpose_rows(("cT", l), lambda t, k: big[:, t, C_DQ + k * P:C_DQ + (k + 1) * P], 3)
                pe.wait_ge(*emptied((("cT", l), 2)))
                product(("uq", l), hT_at, 2, [384], 2)
                product(("ukv", l), lambda k, t: hT_at(2, t), 1, [512], 1)
                pe.wait_ge(*L.next("c_rotated", 2))
                head_transposes(("cqT", l), hd(0, 4, 96))
                head_transposes(("ckT", l),
                                [lambda t, i=i: big[:, t, B_Q + i * 128:B_Q + i * 128 + NOPE] for i in range(4)])
                head_transposes(("krT", l), [lambda t: k_rope[:, t, :]])
                pe.wait_ge(*emptied((("krT", l), 0)))
                pe.wait_ge(*emptied((("cqT", l), 2)))
                heads(("c", l), [([(hv[0:96, i, :], hv[0:96, 4 + i, :])],
                                  lambda j, i=i: big[:, j, B_Q + i * 128 + NOPE:B_Q + (i + 1) * 128], MLA_V, False)
                                 for i in range(MLA_HEADS)])
                product(("pa", l), yT_at, 2, [1024], 2)
                product(("pb", l), lambda k, t: yT_at(2 + k, t), 4, [1024], 4)
                pe.wait_ge(*emptied((("c", l), "value", 3)))
                product(("pc", l), lambda k, t: yT_at(6 + k, t), 2, [1024], 2)
                pe.wait_ge(*L.next("merged"))
                transpose_rows(("mT", l), lambda t, k: mergedA[:, t, k * P:(k + 1) * P], KD)
                pe.wait_ge(*emptied((("mT", l), KD - 2)))
                product(("o", l), hT_at, KD, [512] * 2, KD)

            def cross(l):
                memory = big_flat[:, 0:2048].rearrange("p (t n) -> p t n", t=NT)
                memT = big_flat[:, 2048:4096].rearrange("p (k t) -> p k t", t=T)
                q = big_flat[:, 4096:6144].rearrange("p (t n) -> p t n", t=NT)
                k = big_flat[:, 6144:8192].rearrange("p (t n) -> p t n", t=NT)
                pe.wait_ge(*L.next("mem_landed", 16))
                transpose_rows(("memT", l), lambda t, kk: memory[:, t, kk * P:(kk + 1) * P], KD)
                pe.wait_ge(*L.next("normed"))
                transpose_rows(("hT", "mem", l), lambda t, kk: h[:, t, kk * P:(kk + 1) * P], KD)
                pe.wait_ge(*emptied((("hT", "mem", l), KD - 2)))
                product(("kv", l), lambda kk, t: memT[:, kk, t * P:(t + 1) * P], KD, [512] * 4, KD)
                product(("q", l), hT_at, KD, [512] * 2, KD)
                pe.wait_ge(*emptied((("kv", l), 3)))
                pe.wait_ge(*emptied((("q", l), 1)))
                transpose_rows(("xkT", l), lambda t, kk: k[:, t, kk * P:(kk + 1) * P], KD)
                transpose_rows(("xqT", l), lambda t, kk: q[:, t, kk * P:(kk + 1) * P], KD)
                pe.wait_ge(*emptied((("xqT", l), KD - 2)))
                heads(("x", l), [([(hv[:, 2 * i + j, :], hv[:, 8 + 2 * i + j, :]) for j in range(2)],
                                  lambda j, i=i: memory[:, j, i * MEM_HD:(i + 1) * MEM_HD], MEM_HD, False)
                                 for i in range(MEM_HEADS)])
                pe.wait_ge(*emptied((("x", l), "value", 3)))
                product(("xo", l), yT_at, KD, [512] * 2, KD)

            def ffn_body(name):
                for c in range(HID_CHUNKS + 1):
                    if c < HID_CHUNKS:
                        s = next_tile()
                        o = begin(pairs, (name, "up", c))
                        for t in range(NT):
                            for k in range(KD):
                                ins = mm(o[:, t, :], hT_at(k, t), weights[:, s, k * 512:(k + 1) * 512],
                                                start=(k == 0), stop=(k == KD - 1))
                        end(ins)
                        slot_owed[0] = f"slot{s}_used"
                    if c:
                        pe.wait_ge(*emptied((name, "up", c - 1)))
                        o = begin(banks, (name, "hidT", c - 1))
                        for i in range(2):
                            for t in range(NT):
                                at = (i * NT + t) * P
                                ins = mm_t(o[:, at:at + P], hid[:, (c - 1) % 2, t, i * P:(i + 1) * P], ident)
                        end(ins)
                pe.wait_ge(*emptied((name, "hidT", HID_CHUNKS - 1)))
                pe.wait_ge(*emptied((name, "hidT", HID_CHUNKS - 2)))
                outs = [begin(pairs, (name, "down", i)) for i in range(2)]
                k0 = 0
                for g, nk in enumerate(DOWN_GROUPS):
                    s = next_tile()
                    for i in range(2):
                        for t in range(NT):
                            for k in range(nk):
                                at = k * 1024 + 512 * i
                                ins = mm(outs[i][:, t, :], hidT[:, k0 + k, t * P:(t + 1) * P],
                                                weights[:, s, at:at + 512],
                                                start=(k0 + k == 0), stop=(k0 + k == KF - 1))
                        if g == len(DOWN_GROUPS) - 1 and i == 0:
                            end(ins)
                    ins.then_inc(sems(f"slot{s}_used"), 1)
                    k0 += nk
                pe.wait_ge(*L.at(f"slot{s}_used", tiles_used_at(s)))
                pe.sem_inc(sems("banks_filled"), 1)

            def loop_experts(n, name):
                before = (filled[0], list(pairs.uses), list(banks.uses), tiles_used[0])
                pairs.next = banks.next = 0
                if n == 1:
                    ffn_body(name)
                else:
                    with L.loop(n, PER_EXPERT):
                        ffn_body(name)
                assert filled[0] - before[0] == PER_EXPERT["banks_filled"]
                more = n - 1
                filled[0] += more * (filled[0] - before[0])
                for ring, b in ((pairs, before[1]), (banks, before[2])):
                    for i in range(ring.n):
                        step = ring.uses[i] - b[i]
                        assert PER_EXPERT[ring.emptied(i)] == step, (ring.name, i, step)
                        ring.uses[i] += more * step
                tiles_used[0] += more * (tiles_used[0] - before[3])
                pairs.next = banks.next = 0

            def ffn(l):
                pe.wait_ge(*L.next("normed"))
                transpose_rows(("hT", "ffn", l), lambda t, k: h[:, t, k * P:(k + 1) * P], KD)
                if l == 1:
                    pe.wait_ge(*L.next("router_landed", 16))
                pe.wait_ge(*emptied((("hT", "ffn", l), KD - 2)))
                if l == 1:
                    o = begin(banks, ("router", l))
                    for t in range(NT):
                        for k in range(KD):
                            ins = mm(o[:, t * 8:t * 8 + 8], hT_at(k, t), router_w[:, k, :],
                                            start=(k == 0), stop=(k == KD - 1))
                    end(ins)
                loop_experts(1 if l == 0 else N_EXPERTS, ("ffn", l))

            def even():
                pe.wait_ge(*L.next("normed", 2))
                xn = att[:, 0:2048].rearrange("p (t n) -> p t n", t=NT)
                transpose_rows(("eT",), lambda t, k: xn[:, t, k * P:(k + 1) * P], KD)
                pe.wait_ge(*emptied((("eT",), KD - 2)))
                product(("ez",), hT_at, KD, [512] * 10, KD)
                pe.wait_ge(*L.next("e_rotated", 2))
                hv = att[:, 0:2048].rearrange("p (n t) -> p n t", t=T)
                for g in range(4):
                    head_transposes(("ehT", g),
                                    [lambda t, i=i: e(t, E_Q + (4 * g + i) * HD, HD) for i in range(4)]
                                    + [lambda t, i=i: e(t, E_K + (4 * g + i) * HD, HD) for i in range(4)])
                    pe.wait_ge(*emptied((("ehT", g), 6)))
                    pe.wait_ge(*emptied((("ehT", g), 4)))
                    heads(("e", g), [([(hv[0:HD, i, :], hv[0:HD, 4 + i, :])],
                                      lambda j, i=i: e(j, E_V + (4 * g + i) * HD, HD), HD, True)
                                     for i in range(4)])
                transpose_rows(("uT",), lambda t, k: e(t, E_U + k * P, P), 4)
                uT = hT
                pe.wait_ge(*emptied((("uT",), 2)))
                pe.wait_ge(*L.next("ssm_w_landed", 16))
                y = begin(pairs, ("ssm_y",), late=True)
                for b in range(SSM_TILES // 2 + 1):
                    if b < SSM_TILES // 2:
                        for part in range(2):
                            o = begin(banks, ("Bu", b, part))
                            for i in range(2):
                                j = TILE_AT[2 * b + i]
                                q0 = 32 * (j % 4)
                                ins = mm(o[:, i * T:(i + 1) * T],
                                                ssm_b[q0:q0 + 32, part, j // 4, :],
                                                uT[q0:q0 + 32, j // 4, :], start=True, stop=True,
                                                tile_position=(q0, 0))
                            end(ins)
                    if b:
                        pe.wait_ge(*L.next("states_ready"))
                        for i in range(2):
                            m = 2 * (b - 1) + i
                            j = TILE_AT[m]
                            for t in range(NT):
                                for part in range(2):
                                    ins = mm(y[:, t, 32 * j:32 * j + 32],
                                                    ssm_state[:, part, i, t * P:(t + 1) * P],
                                                    ssm_c[:, part, m, :], start=(part == 0), stop=(part == 1),
                                                    skip_group_check=True)
                        if b == SSM_TILES // 2:
                            end_late(ins, ("ssm_y",))
                        else:
                            ins.then_inc(sems("states_used"), 1)
                pe.wait_ge(*L.next("gelu_done"))
                transpose_rows(("gT",), lambda t, k: e(t, E_U + k * P, P), 4)
                pe.wait_ge(*emptied((("gT",), 2)))
                product(("glu",), hT_at, 4, [512], 4)
                pe.wait_ge(*L.next("even_merged"))
                mT = att[:, 0:3072].rearrange("p (k t) -> p k t", t=T)
                transpose_rows(("emT",), lambda t, k: e(t, E_G + k * P, P), 12)
                pe.wait_ge(*emptied((("emT",), 10)))
                product(("eo",), lambda k, t: mT[:, k, t * P:(t + 1) * P], 12, [512] * 2, 6)

            def odd():
                pe.wait_ge(*L.next("normed", 2))
                xn = att[:, 0:2048].rearrange("p (t n) -> p t n", t=NT)
                transpose_rows(("dT",), lambda t, k: xn[:, t, k * P:(k + 1) * P], KD)
                pe.wait_ge(*emptied((("dT",), KD - 2)))
                product(("dz",), hT_at, KD, [512] * 8, KD)
                u = big_flat[:, 0:4096].rearrange("p (t n) -> p t n", t=NT)
                g = big_flat[:, 4096:8192].rearrange("p (t n) -> p t n", t=NT)
                pe.wait_ge(*L.next("window_landed", 16))
                pe.wait_ge(*emptied((("dz",), 3)))
                mixT = att[:, 0:4096].rearrange("p (k t) -> p k t", t=T)
                for j in range(0, 16, 2):
                    o = begin(banks, ("mixT", j))
                    for i in range(2):
                        for s in range(NT):
                            ins = mm(o[:, i * T:(i + 1) * T], u[:, s, (j + i) * P:(j + i + 1) * P],
                                            window[:, j // 4, s, :], start=(s == 0), stop=(s == NT - 1))
                    end(ins)
                pe.wait_ge(*emptied(("mixT", 14)))
                for gi in range(4):
                    product(("pw", gi), lambda k, t: mixT[:, 4 * gi + k, t * P:(t + 1) * P], 4, [512], 4)
                pe.wait_ge(*L.next("odd_gated"))
                transpose_rows(("odT",), lambda t, k: g[:, t, k * P:(k + 1) * P], 16)
                pe.wait_ge(*emptied((("odT",), 14)))
                product(("do",), lambda k, t: mixT[:, k, t * P:(t + 1) * P], 16, [512] * 2, 8)

            for l in range(DEPTH):
                if on(f"mix{l}"):
                    mixer(l)
                if on(f"mem{l}"):
                    cross(l)
                if on(f"ffn{l}"):
                    ffn(l)
            if on("even"):
                even()
            if on("odd"):
                odd()

        def consumer(L):
            def filled(name):
                return L.at("banks_filled", jobs[name][2])

            def bank(name):
                ring, b, _, _ = jobs[name]
                return ring.views[b], sems(ring.emptied(b))

            def emptied(name):
                ring, b, _, use = jobs[name]
                return L.at(ring.emptied(b), use)
            return filled, bank, emptied

        def bc(ap, axis, shape):
            return ap.unsqueeze(axis).to_broadcast(shape)

        @block.vector
        def _(ve):
            L = Line(ve, sems)
            filled, bank, emptied = consumer(L)
            norms = [0]

            def link(ins):
                ins.then_inc(sems("vector_step"), 1)
                ve.wait_ge(*L.next("vector_step"))

            def copy(name, dst, src=lambda o: o[:, :, :]):
                ve.wait_ge(*filled(name))
                o, free = bank(name)
                ve.tensor_copy(dst, src(o)).then_inc(free, 1)

            def copies(name, dst, k_tiles):
                for j in range(0, k_tiles, 2):
                    n = min(2, k_tiles - j)
                    copy((name, j), dst[:, j:j + n, :],
                         lambda o: o[:, 0:n * T].rearrange("p (k t) -> p k t", t=T))

            def head_copies(name, first, rows, n):
                for j in range(0, n, 2):
                    copy((name, j), hv[0:rows, first + j:first + j + 2, :],
                         lambda o: o[0:rows, :].rearrange("p (k t) -> p k t", t=T))

            def row_stats(src):
                for t in range(NT):
                    for s in range(2):
                        ins = ve.bn_stats(stats[:, t, s, :], src[:, t, 512 * s:512 * s + 512])
                link(ins)
                for t in range(NT):
                    ins = ve.bn_aggr(mv[:, t, :], stats[:, t, :, :])
                link(ins)

            def norm_slot():
                s = norms[0] % 2
                norms[0] += 1
                ve.wait_ge(*L.next(f"norm_par{s}_landed", 16))
                return norm_par[:, s, 0, :], norm_par[:, s, 1, :]

            def inverse_root(v, eps, scale=1.0, src=None):
                ve.tensor_scalar(v, v if src is None else src, scale, eps, ALU.mult, ALU.add)\
                  .then_inc(sems("variance_ready"), 1)
                ve.wait_ge(*L.next("root_ready"))
                link(ve.reciprocal(v, v))

            def layer_norm():
                row_stats(h)
                inverse_root(rstd[:, :, 0], LN_EPS, src=mv[:, :, 1])
                for t in range(NT):
                    ins = ve.tensor_scalar(h[:, t, :], h[:, t, :], mv[:, t, 0:1], rstd[:, t, 0:1],
                                           ALU.subtract, ALU.mult)
                link(ins)
                g, b = norm_slot()
                link(ve.tensor_tensor(h[:, :, :], h[:, :, :], bc(g, 1, [P, NT, D]), ALU.mult))
                ve.tensor_tensor(h[:, :, :], h[:, :, :], bc(b, 1, [P, NT, D]), ALU.add).then_inc(sems("normed"), 1)
                ve.wait_ge(*L.next("normed"))

            def rms_rstd(src):
                row_stats(src)
                link(ve.tensor_tensor(rstd[:, :, 1], mv[:, :, 0], mv[:, :, 0], ALU.mult))
                link(ve.tensor_tensor(rstd[:, :, 1], rstd[:, :, 1], mv[:, :, 1], ALU.add))
                inverse_root(rstd[:, :, 0], RMS_EPS, src=rstd[:, :, 1])

            def pre_norm():
                rms_rstd(h)
                g, _ = norm_slot()
                for t in range(NT):
                    ins = ve.scalar_tensor_tensor(mergedA[:, t, :], h[:, t, :], rstd[:, t, 0:1], g,
                                                  ALU.mult, ALU.mult)
                ins.then_inc(sems("normed"), 1)
                ve.wait_ge(*L.next("normed"))

            def post_norm(name):
                for c in range(2):
                    copy((name, c), y_out[:, :, 512 * c:512 * c + 512])
                ve.wait_ge(*emptied((name, 0)))
                ve.wait_ge(*emptied((name, 1)))
                rms_rstd(y_out)
                g, _ = norm_slot()
                for t in range(NT):
                    ins = ve.scalar_tensor_tensor(y_out[:, t, :], y_out[:, t, :], rstd[:, t, 0:1], g,
                                                  ALU.mult, ALU.mult)
                link(ins)
                ve.tensor_tensor(h[:, :, :], h[:, :, :], y_out, ALU.add).then_inc(sems("normed"), 1)
                ve.wait_ge(*L.next("normed"))

            def residual(name):
                for c in range(2):
                    ve.wait_ge(*filled((name, c)))
                    o, free = bank((name, c))
                    hc = h[:, :, 512 * c:512 * c + 512]
                    ve.scalar_tensor_tensor(hc, hc, ALPHA, o[:, :, :], ALU.mult, ALU.add).then_inc(free, 1)
                ve.wait_ge(*emptied((name, 0)))
                ve.wait_ge(*emptied((name, 1)))

            def rope(x1, x2, d1, d2, cos, sin, t1, t2, done):
                ve.tensor_tensor(t1, x1, cos, ALU.mult)
                link(ve.tensor_tensor(t2, x1, sin, ALU.mult))
                ve.tensor_tensor(d1, x2, sin, ALU.mult)
                link(ve.tensor_tensor(d2, x2, cos, ALU.mult))
                ve.tensor_tensor(d1, t1, d1, ALU.subtract)
                return ve.tensor_tensor(d2, d2, t2, ALU.add).then_inc(sems(done), 1)

            def heads(name, n, store, scale=1.0, mask=None, weight=None):
                for i in range(n + 2):
                    if i < n:
                        ve.wait_ge(*filled((name, "score", i)))
                        o, free = bank((name, "score", i))
                        s = o[:, :].rearrange("p (t k) -> p t k", t=NT)
                        if mask is not None:
                            ve.scalar_tensor_tensor(prob[:, i % 2, :, :], s, scale, mask(i), ALU.mult, ALU.add)\
                              .then_inc(free, 1)
                            ve.wait_ge(*emptied((name, "score", i)))
                            ve.tensor_reduce(smax[:, i % 2, :], prob[:, i % 2, :, :], AX.X, ALU.max, negate=True)\
                              .then_inc(sems("max_ready"), 1)
                        else:
                            link(ve.tensor_reduce(smax[:, i % 2, :], s, AX.X, ALU.max, negate=True))
                            ve.tensor_scalar(smax[:, i % 2, :], smax[:, i % 2, :], scale, None, ALU.mult)\
                              .then_inc(sems("max_ready"), 1)
                    if 1 <= i <= n:
                        m = i - 1
                        if mask is None:
                            ve.wait_ge(*emptied((name, "score", m)))
                        else:
                            ve.wait_ge(*L.next("exp_done"))
                        if weight is None:
                            link(ve.reciprocal(rsum[:, m % 2, :], ssum[:, m % 2, :]))
                            ve.tensor_tensor(prob[:, m % 2, :, :], prob[:, m % 2, :, :],
                                             bc(rsum[:, m % 2, :], 2, [P, NT, T]), ALU.mult)\
                              .then_inc(sems("prob_ready"), 1)
                            L.passed("prob_ready")
                        else:
                            ve.tensor_tensor(prob[:, m % 2, :, :], prob[:, m % 2, :, :], weight, ALU.mult)\
                              .then_inc(sems("prob_ready"), 1)
                            ve.wait_ge(*L.next("prob_ready"))
                            link(ve.tensor_reduce(ssum[:, m % 2, :], prob[:, m % 2, :, :], AX.X, ALU.add))
                            link(ve.reciprocal(rsum[:, m % 2, :], ssum[:, m % 2, :]))
                        copy((name, "probT", m), probT[:, m % 2, :, :],
                             lambda o: o[:, :].rearrange("p (j t) -> p j t", j=NT))
                    if i >= 2:
                        store((name, "value", i - 2), i - 2)

            def store_T(first):
                def store(name, m):
                    copy(name, yT[HD * (m % 2):HD * (m % 2) + HD, first + m // 2, :], lambda o: o[0:HD, 0:T])
                return store

            def mixer(l):
                copies(("hT", "mix", l), hT, KD)
                at = 0
                for c in range(4):
                    w = Z_WIDTHS[c]
                    copy((("z", l), c), big[:, :, at:at + w], lambda o: o[:, :, 0:w])
                    at += w
                for c in range(2, 4):
                    ve.wait_ge(*emptied((("z", l), c)))
                ve.wait_ge(*L.next("head_gain_landed", 16))
                sq = att[:, 2560:2560 + NT * 640].rearrange("p (t n w) -> p t n w", t=NT, w=HD)
                zb = big[:, :, B_Q:B_Q + 640].rearrange("p t (n w) -> p t n w", w=HD)
                gb = head_gain[:, 0:640].rearrange("p (n w) -> p n w", w=HD)
                link(ve.tensor_tensor(sq, zb, zb, ALU.mult))
                link(ve.tensor_reduce(rstd[:, :, 0:10], sq, AX.X, ALU.add))
                inverse_root(rstd[:, :, 0:10], RMS_EPS, 1.0 / HD)
                for t in range(NT):
                    ins = ve.tensor_tensor(zb[:, t, :, :], zb[:, t, :, :], bc(rstd[:, t, 0:10], 2, [P, 10, HD]), ALU.mult)
                link(ins)
                for t in range(NT):
                    ins = ve.tensor_tensor(zb[:, t, :, :], zb[:, t, :, :], gb, ALU.mult)
                link(ins)
                tr = [att[:, 2560 + 320 * i:2560 + 320 * (i + 1)].rearrange("p (n w) -> p n w", w=32) for i in range(4)]
                cb, sn = table(C_COSB, 32), table(C_SINB, 32)
                for t in range(NT):
                    rope(zb[:, t, :, 0:32], zb[:, t, :, 32:64], zb[:, t, :, 0:32], zb[:, t, :, 32:64],
                         bc(cb[:, t, :], 1, [P, 10, 32]), bc(sn[:, t, :], 1, [P, 10, 32]), tr[2 * t], tr[2 * t + 1],
                         "b_rotated")
                ve.wait_ge(*L.next("b_rotated", 2))
                zc = big[:, :, C_DQ:C_DQ + DQ + DKV]
                sqc = att[:, 2560:2560 + NT * 384].rearrange("p (t n) -> p t n", t=NT)
                link(ve.tensor_tensor(sqc, zc, zc, ALU.mult))
                ve.tensor_reduce(rstd[:, :, 10], sqc[:, :, 0:DQ], AX.X, ALU.add)
                link(ve.tensor_reduce(rstd[:, :, 11], sqc[:, :, DQ:DQ + DKV], AX.X, ALU.add))
                link(ve.tensor_scalar(rstd[:, :, 11], rstd[:, :, 11], DQ / DKV, None, ALU.mult))
                inverse_root(rstd[:, :, 10:12], RMS_EPS, 1.0 / DQ)
                for t in range(NT):
                    for c, (a, w) in enumerate(((0, DQ), (DQ, DKV))):
                        ins = ve.scalar_tensor_tensor(zc[:, t, a:a + w], zc[:, t, a:a + w], rstd[:, t, 10 + c:11 + c],
                                                      head_gain[:, 640 + a:640 + a + w], ALU.mult, ALU.mult)
                ins.then_inc(sems("c_normed"), 1)
                ve.wait_ge(*L.next("c_normed"))
                cc, sc = table(C_COSC, 16), table(C_SINC, 16)
                tk = [att[:, 2560 + 32 * i:2592 + 32 * i].rearrange("p (t w) -> p t w", t=NT) for i in range(2)]
                kr = big[:, :, C_KR:C_KR + ROPE_C]
                rope(kr[:, :, 0:16], kr[:, :, 16:32], k_rope[:, :, 0:16], k_rope[:, :, 16:32], cc, sc, tk[0], tk[1],
                     "k_rotated")

                head_copies(("aT", l), 0, HD, 8)

                def head_bias(i):
                    ve.wait_ge(*L.next(f"bias{i % 2}_landed", 16))
                    return bias[:, i % 2, :, :]
                heads(("a", l), NA_HEADS, store_T(0), HD ** -0.5, mask=head_bias)
                head_copies(("bT", l), 0, HD, 10)
                heads(("b", l), GQA_HEADS, store_T(2), HD ** -0.5)
                copies(("cT", l), hT, 3)
                copy((("uq", l), 0), big[:, :, 0:384], lambda o: o[:, :, 0:384])
                copy((("ukv", l), 0), big[:, :, B_Q:B_Q + 512])
                ve.wait_ge(*emptied((("uq", l), 0)))
                qc = big[:, :, 0:384].rearrange("p t (n w) -> p t n w", w=96)
                tq = [att[:, 2560 + 64 * i:2624 + 64 * i].rearrange("p (n w) -> p n w", w=16) for i in range(4)]
                for t in range(NT):
                    rope(qc[:, t, :, 64:80], qc[:, t, :, 80:96], qc[:, t, :, 64:80], qc[:, t, :, 80:96],
                         bc(cc[:, t, :], 1, [P, 4, 16]), bc(sc[:, t, :], 1, [P, 4, 16]), tq[2 * t], tq[2 * t + 1],
                         "c_rotated")
                head_copies(("cqT", l), 0, 96, 4)
                head_copies(("ckT", l), 4, NOPE, 4)
                copy((("krT", l), 0), hv[64:96, 4:8, :], lambda o: bc(o[0:32, 0:T], 1, [32, 4, T]))
                heads(("c", l), MLA_HEADS, store_T(6), (NOPE + ROPE_C) ** -0.5)
                for b, branch in enumerate(("pa", "pb", "pc")):
                    for c in range(2):
                        g = big[:, :, ZQ + b * D + 512 * c:ZQ + b * D + 512 * c + 512]
                        ve.wait_ge(*emptied((("z", l), 4 + 2 * b + c)))
                        ve.wait_ge(*filled(((branch, l), c)))
                        o, free = bank(((branch, l), c))
                        m = mergedA[:, :, 512 * c:512 * c + 512]
                        if b == 0:
                            ve.tensor_tensor(m, g, o[:, :, :], ALU.mult).then_inc(free, 1)
                        else:
                            ve.tensor_tensor(g, g, o[:, :, :], ALU.mult).then_inc(free, 1)
                            ve.wait_ge(*emptied(((branch, l), c)))
                            ins = ve.tensor_tensor(m, m, g, ALU.add)
                            if (b, c) == (2, 1):
                                ins.then_inc(sems("merged"), 1)
                            else:
                                link(ins)
                copies(("mT", l), hT, KD)
                residual(("o", l))
                layer_norm()

            def cross(l):
                memory = big_flat[:, 0:2048].rearrange("p (t n) -> p t n", t=NT)
                memT = big_flat[:, 2048:4096].rearrange("p (k t) -> p k t", t=T)
                q = big_flat[:, 4096:6144].rearrange("p (t n) -> p t n", t=NT)
                k = big_flat[:, 6144:8192].rearrange("p (t n) -> p t n", t=NT)
                copies(("memT", l), memT, KD)
                copies(("hT", "mem", l), hT, KD)
                for c in range(4):
                    dst = k if c < 2 else memory
                    copy((("kv", l), c), dst[:, :, 512 * (c % 2):512 * (c % 2) + 512])
                for c in range(2):
                    copy((("q", l), c), q[:, :, 512 * c:512 * c + 512])
                copies(("xkT", l), hv[:, 8:16, :], KD)
                copies(("xqT", l), hv[:, 0:8, :], KD)

                def store(name, m):
                    copy(name, yT[:, 2 * m:2 * m + 2, :], lambda o: o[:, :].rearrange("p (k t) -> p k t", t=T))
                heads(("x", l), MEM_HEADS, store, MEM_HD ** -0.5)
                residual(("xo", l))
                layer_norm()

            def route():
                ve.wait_ge(*filled(("router", 1)))
                o, free = bank(("router", 1))
                ve.tensor_copy(logit[:, :, :], o[:, 0:NT * 8].rearrange("p (t n) -> p t n", t=NT)).then_inc(free, 1)
                ve.wait_ge(*emptied(("router", 1)))
                for t in range(NT):
                    ins = ve.max(top[:, t, :], logit[:, t, :])
                link(ins)
                for t in range(NT):
                    ins = ve.max_index(top_i[:, t, :], top[:, t, :], logit[:, t, :])
                link(ins)
                ve.tensor_copy(top_f[:, :, :], top_i[:, :, :])
                ve.tensor_tensor(rstd[:, :, 0], top[:, :, 1], top[:, :, 0], ALU.subtract)\
                  .then_inc(sems("top_gap"), 1)
                ve.wait_ge(*L.next("second_exp"))
                link(ve.tensor_scalar(rstd[:, :, 2], rstd[:, :, 1], 1.0, None, ALU.add))
                link(ve.reciprocal(rstd[:, :, 3], rstd[:, :, 2]))
                link(ve.tensor_tensor(rstd[:, :, 4], rstd[:, :, 1], rstd[:, :, 3], ALU.mult))
                iota8 = const[:, C_IOTA8:C_IOTA8 + 8]
                for t in range(NT):
                    ve.tensor_scalar(tmp8[:, t, :], iota8, top_f[:, t, 0:1], rstd[:, t, 3:4], ALU.is_equal, ALU.mult)
                    ins = ve.tensor_scalar(gate[:, t, 0:8], iota8, top_f[:, t, 1:2], rstd[:, t, 4:5],
                                           ALU.is_equal, ALU.mult)
                link(ins)
                link(ve.tensor_tensor(gate[:, :, 0:8], gate[:, :, 0:8], tmp8[:, :, :], ALU.add))

            def ffn_body(name, col):
                for c in range(HID_CHUNKS + 1):
                    if c < HID_CHUNKS:
                        ve.wait_ge(*L.next("silu_done"))
                        ve.wait_ge(*filled((name, "up", c)))
                        o, free = bank((name, "up", c))
                        ve.tensor_tensor(hid[:, c % 2, :, :], silu[:, c % 2, :, :], o[:, :, 256:512], ALU.mult)\
                          .then_inc(free, 1)
                    if c:
                        copy((name, "hidT", c - 1), hidT[:, 2 * c - 2:2 * c, :],
                             lambda o: o[:, :].rearrange("p (k t) -> p k t", t=T))
                for i in range(2):
                    ve.wait_ge(*filled((name, "down", i)))
                    o, free = bank((name, "down", i))
                    for t in range(NT):
                        hc = h[:, t, 512 * i:512 * i + 512]
                        ins = ve.scalar_tensor_tensor(hc, o[:, t, :], gate[:, t, col], hc, ALU.mult, ALU.add)
                    ins.then_inc(free, 1)

            def ffn(l):
                copies(("hT", "ffn", l), hT, KD)
                link(ve.tensor_scalar(h[:, :, :], h[:, :, :], ALPHA, None, ALU.mult))
                name = ("ffn", l)
                if l == 0:
                    link(ve.memset(gate[:, :, 8:9], 1.0))
                    ffn_body(name, slice(8, 9))
                else:
                    route()
                    with L.loop(N_EXPERTS, PER_EXPERT) as ex:
                        ffn_body(name, bass.ds(ex, 1))
                for i in range(2):
                    ring, b, _, use = jobs[(name, "down", i)]
                    ve.wait_ge(*L.at(ring.emptied(b), use + (0 if l == 0 else (N_EXPERTS - 1) * PER_EXPERT[ring.emptied(b)])))
                layer_norm()

            def even():
                pre_norm()
                copies(("eT",), hT, KD)
                for c in (0, 1, 2, 3, 4, 5, 8):
                    copy((("ez",), c), wide[:, :, 512 * c:512 * c + 512])
                ve.wait_ge(*emptied((("ez",), 3)))
                qk = wide[:, :, 0:2048].rearrange("p t (n w) -> p t n w", w=HD)
                t1, t2 = [att[:, 5120 + 256 * i:5376 + 256 * i].rearrange("p (n w) -> p n w", w=8) for i in range(2)]
                t3, t4 = [att[:, 5632 + 256 * i:5888 + 256 * i].rearrange("p (n w) -> p n w", w=8) for i in range(2)]
                c2, s2 = table(C_COS2, 8), table(C_SIN2, 8)
                for t, (ta, tb) in enumerate(((t1, t2), (t3, t4))):
                    rope(qk[:, t, :, 0:8], qk[:, t, :, 8:16], qk[:, t, :, 0:8], qk[:, t, :, 8:16],
                         bc(c2[:, t, :], 1, [P, 32, 8]), bc(s2[:, t, :], 1, [P, 32, 8]), ta, tb, "e_rotated")
                ve.wait_ge(*emptied((("ez",), 6)))
                ve.wait_ge(*emptied((("ez",), 7)))
                dmask = table(C_DMASK, T)
                dmul = table(C_DMUL, T)

                for g in range(4):
                    def store(name, m, g=g):
                        ve.wait_ge(*filled(name))
                        o, free = bank(name)
                        for t in range(NT):
                            dst = e(t, E_G + (4 * g + m) * HD, HD)
                            ins = ve.scalar_tensor_tensor(dst, o[:, t * HD:(t + 1) * HD], rsum[:, m % 2, t:t + 1], dst,
                                                          ALU.mult, ALU.mult)
                        ins.then_inc(free, 1)
                    head_copies(("ehT", g), 0, HD, 8)
                    heads(("e", g), 4, store, HD ** -0.5, mask=lambda i: dmask, weight=dmul)
                copies(("uT",), hT, 4)
                ssm()
                copies(("gT",), hT, 4)
                ve.wait_ge(*filled((("glu",), 0)))
                o, free = bank((("glu",), 0))
                z = rot_in_flat
                ve.tensor_tensor(z, o[:, :, :], bc(ssm_vec[:, 1, :], 1, [P, NT, SSM_W]), ALU.add).then_inc(free, 1)
                ve.wait_ge(*L.next("glu_sigmoid"))
                ve.wait_ge(*emptied((("ez",), 9)))
                u = wide[:, :, E_U:E_U + SSM_W]
                link(ve.tensor_tensor(u, u, z, ALU.mult))
                ve.tensor_tensor(u, u, wide[:, :, E_GS:E_GS + SSM_W], ALU.mult).then_inc(sems("even_merged"), 1)
                copies(("emT",), att[:, 0:3072].rearrange("p (k t) -> p k t", t=T), 12)
                post_norm(("eo",))

            rot_in_flat = big_flat[:, 2048:3072].rearrange("p (t n) -> p t n", t=NT)

            def ssm():
                ve.wait_ge(*L.next("ssm_par_landed", 16))
                a_re, a_im = ssm_par[:, 0, :], ssm_par[:, 1, :]
                V = [ssm_s[:, i, :] for i in range(16)]
                dt, re, im, rho, tau, k, sn, cs, lr, li, den, cr, ci, x, y2, th = V

                def tt(o, a, b, op):
                    link(ve.tensor_tensor(o, a, b, op))

                def ts(o, a, s1, op1, s2=None, op2=ALU.bypass):
                    link(ve.tensor_scalar(o, a, s1, s2, op1, op2))

                ve.wait_ge(*L.next("ssm_dt"))
                tt(im, a_im, dt, ALU.mult)
                ve.tensor_tensor(re, a_re, dt, ALU.mult).then_inc(sems("ssm_re"), 1)
                ts(k, im, 1 / TWO_PI, ALU.mult)
                ts(k, k, ROUND, ALU.add, ROUND, ALU.subtract)
                link(ve.scalar_tensor_tensor(th, k, -TWO_PI_HI, im, ALU.mult, ALU.add))
                link(ve.scalar_tensor_tensor(th, k, -TWO_PI_LO, th, ALU.mult, ALU.add))
                ts(tau, th, 1 / TWO_PI, ALU.mult)
                ts(x, tau, 0.25, ALU.add)
                ts(k, x, ROUND, ALU.add, ROUND, ALU.subtract)
                ve.tensor_tensor(x, x, k, ALU.subtract).then_inc(sems("ssm_phase"), 1)
                ve.wait_ge(*L.next("ssm_phase"))
                tt(den, a_re, a_re, ALU.mult)
                tt(y2, a_im, a_im, ALU.mult)
                tt(den, den, y2, ALU.add)
                link(ve.reciprocal(den, den))
                ve.wait_ge(*L.next("ssm_lam"))
                tt(lr, rho, cs, ALU.mult)
                tt(li, rho, sn, ALU.mult)
                ts(lr, lr, 1.0, ALU.subtract)
                tt(cr, lr, a_re, ALU.mult)
                tt(y2, li, a_im, ALU.mult)
                tt(cr, cr, y2, ALU.add)
                tt(cr, cr, den, ALU.mult)
                tt(ci, li, a_re, ALU.mult)
                tt(y2, lr, a_im, ALU.mult)
                tt(ci, ci, y2, ALU.subtract)
                tt(ci, ci, den, ALU.mult)
                ve.wait_ge(*L.next("ssm_w_landed", 16))
                ta = tmp_flat(0)
                tb = tmp_flat(1)
                tc = tmp_flat(2)
                cre, cim = ssm_c[:, 0, :, :], ssm_c[:, 1, :, :]
                crb, cib = bc(cr, 2, [P, SSM_TILES, 32]), bc(ci, 2, [P, SSM_TILES, 32])
                tt(ta, cre, cib, ALU.mult)
                tt(tb, cim, crb, ALU.mult)
                tt(ta, ta, tb, ALU.add)
                tt(tb, cre, crb, ALU.mult)
                tt(tc, cim, cib, ALU.mult)
                tt(cre, tb, tc, ALU.subtract)
                ts(cim, ta, -1.0, ALU.mult)
                ve.wait_ge(*L.next("ssm_vec_landed", 16))
                du = mergedA[:, :, 0:SSM_W]
                ve.tensor_tensor(du, wide[:, :, E_U:E_U + SSM_W], bc(ssm_vec[:, 0, :], 1, [P, NT, SSM_W]), ALU.mult)
                time = const[:, C_TIME:C_TIME + T]
                n = SSM_TILES // 2

                def angles(b):
                    f, g = sinT[:, b % 2, :, :], cosT[:, b % 2, :, :]
                    tt(f, bc(time, 1, [P, 2, T]), bc(tau[:, 2 * b:2 * b + 2], 2, [P, 2, T]), ALU.mult)
                    ts(tmpA, f, ROUND, ALU.add, ROUND, ALU.subtract)
                    tt(f, f, tmpA, ALU.subtract)
                    ts(g, f, 0.25, ALU.add)
                    ts(tmpA, g, ROUND, ALU.add, ROUND, ALU.subtract)
                    ve.tensor_tensor(g, g, tmpA, ALU.subtract).then_inc(sems("angles_ready"), 1)
                    ve.wait_ge(*L.next("angles_ready"))

                angles(0)
                for b in range(n):
                    if b + 1 < n:
                        angles(b + 1)
                    ve.wait_ge(*L.next("sincos_ready"))
                    S, C = sinT[:, b % 2, :, :], cosT[:, b % 2, :, :]
                    ve.wait_ge(*filled(("Bu", b, 0)))
                    o_re, free_re = bank(("Bu", b, 0))
                    ve.wait_ge(*filled(("Bu", b, 1)))
                    o_im, free_im = bank(("Bu", b, 1))
                    bre = o_re[:, :].rearrange("p (i t) -> p i t", i=2)
                    bim = o_im[:, :].rearrange("p (i t) -> p i t", i=2)
                    wr, wi = rot_in[:, 0, :, :], rot_in[:, 1, :, :]
                    tt(wr, C, bre, ALU.mult)
                    tt(tmpA, S, bim, ALU.mult)
                    ve.tensor_tensor(wi, C, bim, ALU.mult).then_inc(free_im, 1)
                    ve.tensor_tensor(tmpB, S, bre, ALU.mult).then_inc(free_re, 1)
                    ve.wait_ge(*emptied(("Bu", b, 0)))
                    ve.wait_ge(*emptied(("Bu", b, 1)))
                    tt(wr, wr, tmpA, ALU.add)
                    tt(wi, wi, tmpB, ALU.subtract)
                    for c, w in enumerate((wr, wi)):
                        for i in range(2):
                            j = 2 * b + i
                            ins = ve.tensor_tensor_scan(scanned[:, c, i, :], rho[:, j:j + 1].to_broadcast([P, T]),
                                                        w[:, i, :], 0.0, ALU.mult, ALU.add)
                    link(ins)
                    rr, ri = scanned[:, 0, :, :], scanned[:, 1, :, :]
                    if b:
                        ve.wait_ge(*L.next("states_used"))
                    sr, si = ssm_state[:, 0, :, :], ssm_state[:, 1, :, :]
                    tt(sr, C, rr, ALU.mult)
                    tt(tmpA, S, ri, ALU.mult)
                    tt(si, C, ri, ALU.mult)
                    tt(tmpB, S, rr, ALU.mult)
                    tt(sr, sr, tmpA, ALU.subtract)
                    ve.tensor_tensor(si, si, tmpB, ALU.add).then_inc(sems("states_ready"), 1)
                    ve.wait_ge(*L.next("states_ready"))
                ve.wait_ge(*filled(("ssm_y",)))
                o, free = bank(("ssm_y",))
                ve.tensor_tensor(wide[:, :, E_U:E_U + SSM_W], o[:, :, :], du, ALU.add).then_inc(free, 1)

            def tmp_flat(i):
                return big_flat[:, at1 + 512 * i:at1 + 512 * (i + 1)].rearrange("p (j n) -> p j n", n=32)

            def odd():
                pre_norm()
                copies(("dT",), hT, KD)
                u = big_flat[:, 0:4096].rearrange("p (t n) -> p t n", t=NT)
                g = big_flat[:, 4096:8192].rearrange("p (t n) -> p t n", t=NT)
                for c in range(4):
                    copy((("dz",), c), u[:, :, 512 * c:512 * c + 512])
                copies("mixT", att[:, 0:4096].rearrange("p (k t) -> p k t", t=T), 16)
                ve.wait_ge(*L.next("pool_scale_landed", 16))
                for gi in range(4):
                    ta = att[:, 4096 + 1024 * (gi % 2):5120 + 1024 * (gi % 2)].rearrange("p (t n) -> p t n", t=NT)
                    ve.wait_ge(*filled((("pw", gi), 0)))
                    o, free = bank((("pw", gi), 0))
                    ve.tensor_tensor(ta, o[:, :, :], bc(pool_scale[:, 512 * gi:512 * gi + 512], 1, [P, NT, 512]),
                                     ALU.mult).then_inc(free, 1)
                    ve.wait_ge(*emptied((("pw", gi), 0)))
                    ve.wait_ge(*emptied((("dz",), 4 + gi)))
                    gg = g[:, :, 512 * gi:512 * gi + 512]
                    ins = ve.tensor_tensor(gg, gg, ta, ALU.mult)
                ins.then_inc(sems("odd_gated"), 1)
                copies(("odT",), att[:, 0:4096].rearrange("p (k t) -> p k t", t=T), 16)
                post_norm(("do",))

            ve.wait_ge(*L.next("const_landed", 16))
            ve.wait_ge(*L.next("x_landed", 16))
            layer_norm()
            for l in range(DEPTH):
                if on(f"mix{l}"):
                    mixer(l)
                if on(f"mem{l}"):
                    cross(l)
                if on(f"ffn{l}"):
                    ffn(l)
            if on("even"):
                even()
            if on("odd"):
                odd()

        @block.scalar
        def _(act):
            L = Line(act, sems)
            filled, bank, emptied = consumer(L)

            def exps(name, n, scale, masked):
                for i in range(n):
                    act.wait_ge(*L.next("max_ready"))
                    ring, b, _, _ = jobs[(name, "score", i)]
                    for t in range(NT):
                        p = prob[:, i % 2, t, :]
                        src = p if masked else ring.views[b][:, t * T:(t + 1) * T]
                        ins = act.activation(p, src, ACT.Exp, bias=smax[:, i % 2, t:t + 1],
                                             scale=1.0 if masked else scale, accum_out=ssum[:, i % 2, t:t + 1])
                    ins.then_inc(sems("exp_done") if masked else sems(ring.emptied(b)), 1)

            def root(a=0, b=1):
                act.wait_ge(*L.next("variance_ready"))
                act.activation(rstd[:, :, a:b], rstd[:, :, a:b], ACT.Sqrt).then_inc(sems("root_ready"), 1)

            def gates(name, chunks, func, dst):
                for c in chunks:
                    act.wait_ge(*filled((name, c)))
                    o, free = bank((name, c))
                    act.activation(dst(c), o[:, :, :], func).then_inc(free, 1)

            def ffn_body(name):
                for c in range(HID_CHUNKS):
                    act.wait_ge(*filled((name, "up", c)))
                    o, _ = bank((name, "up", c))
                    act.activation(silu[:, c % 2, :, :], o[:, :, 0:256], ACT.Silu).then_inc(sems("silu_done"), 1)

            root()
            for l in range(DEPTH):
                if on(f"mix{l}"):
                    root(0, 10)
                    root(10, 12)
                    gates(("z", l), range(4, 10), ACT.Sigmoid,
                          lambda c: big[:, :, ZQ + 512 * (c - 4):ZQ + 512 * (c - 3)])
                    exps(("a", l), NA_HEADS, 1.0, True)
                    exps(("b", l), GQA_HEADS, HD ** -0.5, False)
                    exps(("c", l), MLA_HEADS, (NOPE + ROPE_C) ** -0.5, False)
                    root()
                if on(f"mem{l}"):
                    exps(("x", l), MEM_HEADS, MEM_HD ** -0.5, False)
                    root()
                if on(f"ffn{l}"):
                    if l == 0:
                        ffn_body(("ffn", l))
                    else:
                        act.wait_ge(*L.next("top_gap"))
                        act.activation(rstd[:, :, 1], rstd[:, :, 0], ACT.Exp).then_inc(sems("second_exp"), 1)
                        with L.loop(N_EXPERTS, PER_EXPERT):
                            ffn_body(("ffn", l))
                    root()
            if on("even"):
                root()
                gates(("ez",), (6, 7, 9), ACT.Silu, lambda c: wide[:, :, 512 * c:512 * c + 512])
                for g in range(4):
                    exps(("e", g), 4, 1.0, True)
                dt, re, im, rho, tau, k, sn, cs = [ssm_s[:, i, :] for i in range(8)]
                x, th = ssm_s[:, 13, :], ssm_s[:, 15, :]
                act.wait_ge(*L.next("ssm_par_landed", 16))
                act.activation(dt, ssm_par[:, 2, :], ACT.Exp).then_inc(sems("ssm_dt"), 1)
                act.wait_ge(*L.next("ssm_re"))
                act.activation(rho, re, ACT.Exp)
                act.wait_ge(*L.next("ssm_phase"))
                act.activation(sn, tau, ACT.Sin, scale=TURN)
                act.activation(cs, x, ACT.Sin, scale=TURN).then_inc(sems("ssm_lam"), 1)
                for b in range(SSM_TILES // 2):
                    act.wait_ge(*L.next("angles_ready"))
                    act.activation(sinT[:, b % 2, :, :], sinT[:, b % 2, :, :], ACT.Sin, scale=TURN)
                    act.activation(cosT[:, b % 2, :, :], cosT[:, b % 2, :, :], ACT.Sin, scale=TURN)\
                       .then_inc(sems("sincos_ready"), 1)
                act.wait_ge(*emptied(("ssm_y",)))
                u = wide[:, :, E_U:E_U + SSM_W]
                act.activation(u, u, ACT.Gelu_apprx_tanh).then_inc(sems("gelu_done"), 1)
                act.wait_ge(*emptied((("glu",), 0)))
                z = big_flat[:, 2048:3072].rearrange("p (t n) -> p t n", t=NT)
                act.activation(z, z, ACT.Sigmoid).then_inc(sems("glu_sigmoid"), 1)
                root()
            if on("odd"):
                root()
                g = big_flat[:, 4096:8192].rearrange("p (t n) -> p t n", t=NT)
                gates(("dz",), range(4, 8), ACT.Silu, lambda c: g[:, :, 512 * (c - 4):512 * (c - 3)])
                root()

        @block.gpsimd
        def _(gp):
            L = Line(gp, sems)
            filled, bank, emptied = consumer(L)
            rows = d["x"].rearrange("(t p) n -> p t n", p=P)
            gp.dma_start(h[:, :, :], rows).then_inc(sems("x_landed"), 16)
            norms = [0]

            def norm_params():
                n = norms[0]
                norms[0] += 1
                if n >= 2:
                    gp.wait_ge(*L.at("normed", n - 1))
                gp.dma_start(norm_par[:, n % 2, :, :].rearrange("p a n -> p (a n)"),
                             d["norms"][n:n + 1, :].to_broadcast([P, 2 * D])).then_inc(sems(f"norm_par{n % 2}_landed"), 16)

            norm_params()
            gp.dma_start(const[:, :], d["const"]).then_inc(sems("const_landed"), 16)
            norm_params()
            gp.dma_start(router_w[:, :, :], d["router"].rearrange("p (k n) -> p k n", n=N_EXPERTS))\
              .then_inc(sems("router_landed"), 16)
            gp.dma_start(ssm_par[:, :, :], d["ssm_par"].rearrange("p (c j) -> p c j", c=3))\
              .then_inc(sems("ssm_par_landed"), 16)
            for l in range(DEPTH):
                if on(f"mix{l}"):
                    if l:
                        gp.wait_ge(*L.at("normed", 2))
                    gp.dma_start(head_gain[:, :], d["head_gain"][l:l + 1, :].to_broadcast([P, 1024]))\
                      .then_inc(sems("head_gain_landed"), 16)
                    for i in range(NA_HEADS):
                        if i >= 2:
                            gp.wait_ge(*emptied((("a", l), "score", i - 2)))
                        elif l:
                            gp.wait_ge(*emptied((("a", l - 1), "score", i + 2)))
                        gp.dma_start(bias[:, i % 2, :, :], d["bias"][l, i].rearrange("p (t k) -> p t k", t=NT))\
                          .then_inc(sems(f"bias{i % 2}_landed"), 16)
                    norm_params()
                if on(f"mem{l}"):
                    gp.wait_ge(*L.at("merged", l + 1))
                    gp.dma_start(big_flat[:, 0:2048].rearrange("p (t n) -> p t n", t=NT),
                                 d["mem"].rearrange("(t p) n -> p t n", p=P)).then_inc(sems("mem_landed"), 16)
                    norm_params()
                if on(f"ffn{l}"):
                    norm_params()
            if on("even"):
                gp.wait_ge(*L.at("normed", 7))
                gp.dma_start(att[:, 2048:4096], d["ssm_w"]).then_inc(sems("ssm_w_landed"), 16)
                gp.dma_start(att[:, 4096:5120], d["ssm_vec"][0:1, :].to_broadcast([P, 1024]))\
                  .then_inc(sems("ssm_vec_landed"), 16)
                norm_params()
                norm_params()
            if on("odd"):
                gp.wait_ge(*L.at("normed", 9))
                gp.dma_start(att[:, 4096:6144], d["window"]).then_inc(sems("window_landed"), 16)
                gp.dma_start(pool_scale, d["pool_scale"][0:1, :].to_broadcast([P, POOL_W]))\
                  .then_inc(sems("pool_scale_landed"), 16)
                norm_params()

        @block.sync
        def _(sp):
            L = Line(sp, sems)
            n = [0]

            def load(src, width):
                i = n[0]
                n[0] += 1
                s = i % NSLOT
                if i >= NSLOT:
                    sp.wait_ge(*L.at(f"slot{s}_used", i // NSLOT))
                sp.dma_start(weights[:, s, 0:width], src).then_inc(sems(f"slot{s}_landed"), 16)

            def stream(src, k_tiles, widths, group):
                for c, k0, nk, w, off in weight_tiles(k_tiles, widths, group):
                    load(src[:, off:off + nk * w], nk * w)

            def expert(up, down):
                for c in range(HID_CHUNKS):
                    load(up[:, c * 4096:(c + 1) * 4096], 4096)
                k0 = 0
                for nk in DOWN_GROUPS:
                    load(down[:, k0 * 1024:(k0 + nk) * 1024], nk * 1024)
                    k0 += nk

            for l in range(DEPTH):
                if on(f"mix{l}"):
                    stream(d["w_in"][l], KD, Z_WIDTHS, KD)
                    stream(d["w_uq"][l], 2, [384], 2)
                    stream(d["w_ukv"][l], 1, [512], 1)
                    stream(d["w_pa"][l], 2, [1024], 2)
                    stream(d["w_pb"][l], 4, [1024], 4)
                    stream(d["w_pc"][l], 2, [1024], 2)
                    stream(d["w_out"][l], KD, [512] * 2, KD)
                if on(f"mem{l}"):
                    stream(d["mem_wkv"][l], KD, [512] * 4, KD)
                    stream(d["mem_wq"][l], KD, [512] * 2, KD)
                    stream(d["mem_wo"][l], KD, [512] * 2, KD)
                if on(f"ffn{l}"):
                    if l == 0:
                        expert(d["ffn_up"][0], d["ffn_down"][0])
                    else:
                        before = n[0]
                        with L.loop(N_EXPERTS, PER_EXPERT) as ex:
                            expert(d["moe_up"][bass.ds(ex, 1)].rearrange("e p n -> p (e n)"),
                                   d["moe_down"][bass.ds(ex, 1)].rearrange("e p n -> p (e n)"))
                        n[0] += (N_EXPERTS - 1) * (n[0] - before)
            if on("even"):
                stream(d["even_in"], KD, [512] * 10, KD)
                stream(d["glu"], 4, [512], 4)
                stream(d["even_out"], 12, [512] * 2, 6)
            if on("odd"):
                stream(d["odd_in"], KD, [512] * 8, KD)
                for gi in range(4):
                    stream(d["pool_w"][gi], 4, [512], 4)
                stream(d["odd_out"], 16, [512] * 2, 8)
            assert n[0] == tiles_used[0], (n[0], tiles_used[0])
            n_norms = {"emb": 1, "even": 9, "odd": 11}.get(STAGES[n_stages - 1], n_stages)
            sp.wait_ge(*L.at("normed", n_norms))
            sp.dma_start(out.rearrange("a (t p) n -> p (a t) n", p=P), h[:, :, :]).then_inc(sems("out_stored"), 16)
            sp.wait_ge(sems("out_stored"), 16)


def _packed(w, widths, group):
    k, n = w.shape
    v = w.reshape(k // P, P, n).transpose(1, 0, 2)
    out, at = np.empty((P, k // P * n), w.dtype), 0
    starts = [sum(widths[:c]) for c in range(len(widths))]
    for c, k0, nk, width, off in weight_tiles(k // P, widths, group):
        out[:, off:off + nk * width] = v[:, k0:k0 + nk, starts[c]:starts[c] + width].reshape(P, nk * width)
    return out


def _experts(up, down):
    e = up.shape[0]
    u = up.reshape(e, KD, P, 2, HID_CHUNKS, 256).transpose(0, 2, 4, 1, 3, 5).reshape(e, P, HID_CHUNKS * 4096)
    w = down.reshape(e, KF, P, D).transpose(0, 2, 1, 3).reshape(e, P, KF * D)
    return np.ascontiguousarray(u), np.ascontiguousarray(w)


def _window_index():
    rows = T // GRID_W
    r, c = np.arange(T) // GRID_W, np.arange(T) % GRID_W
    first = np.clip(c - NA_COLS // 2, 0, GRID_W - NA_COLS)
    inside = (c[None, :] >= first[:, None]) & (c[None, :] < first[:, None] + NA_COLS)
    dr = r[None, :] - r[:, None] + 7
    dc = np.clip(c[None, :] - c[:, None] + NA_COLS - 1, 0, 2 * NA_COLS - 2)
    assert rows <= 8
    return inside, dr, dc


def _tiles(a):
    return a.reshape(NT, P, -1).transpose(1, 0, 2).reshape(P, -1)


def _constants():
    c = np.zeros((P, C_END), np.float32)
    c[:, C_ID:C_ID + P] = np.eye(P)
    t = np.arange(T)
    row, col = (t // GRID_W).astype(np.float32), (t % GRID_W).astype(np.float32)

    def axial(rot):
        n = rot // 4
        inv = (np.float32(ROPE_THETA) ** (-np.arange(n, dtype=np.float32) / np.float32(n))).astype(np.float32)
        return np.concatenate([row[:, None] * inv, col[:, None] * inv], axis=-1)
    for at, rot in ((C_COSB, HD), (C_COSC, ROPE_C)):
        ang = axial(rot)
        w = NT * rot // 2
        c[:, at:at + w] = _tiles(np.cos(ang))
        c[:, at + w:at + 2 * w] = _tiles(np.sin(ang))
    inv = (np.float32(THETA_2) ** (-np.arange(0, ROT, 2, dtype=np.float32) / np.float32(ROT))).astype(np.float32)
    ang = t.astype(np.float32)[:, None] * inv
    c[:, C_COS2:C_COS2 + 16] = _tiles(np.cos(ang))
    c[:, C_SIN2:C_SIN2 + 16] = _tiles(np.sin(ang))
    delta = t[:, None] - t[None, :]
    count = sum(((delta >= 0) & (delta <= w) & (delta % dil == 0)).astype(np.float32)
                for w, dil in ((128, 1), (512, 4), (2048, 16)))
    c[:, C_DMASK:C_DMASK + NT * T] = _tiles(np.where(count > 0, 0.0, NEG).astype(np.float32))
    c[:, C_DMUL:C_DMUL + NT * T] = _tiles(count)
    c[:, C_TIME:C_TIME + T] = t
    c[:, C_IOTA8:C_IOTA8 + 8] = np.arange(8)
    return c


def _windows():
    t = np.arange(T)
    out = np.zeros((P, 4, NT, T), np.float32)
    for g, w in enumerate(POOL_WINDOWS):
        d = t[None, :] - t[:, None]
        m = ((d >= 0) & (d < w)) / np.minimum(t[None, :] + 1, w) - (d == 0)
        out[:, g] = m.reshape(NT, P, T).transpose(1, 0, 2)
    return out.reshape(P, -1)


def _layout(i):
    a = {k: np.asarray(v) for k, v in i.items()}
    f = np.float32
    d = {"x": a["x"].reshape(T, D), "mem": a["mem"].reshape(T, D), "const": _constants(), "window": _windows()}
    zero = np.zeros(D, f)
    norms = [(a["emb_ln_g"], a["emb_ln_b"])]
    norms += [(a["ln_g"][l, j], a["ln_b"][l, j]) for l in range(DEPTH) for j in range(3)]
    for l in range(DEPTH):
        norms += [(a["pre_norm_2"][l], zero), (a["post_norm_2"][l], zero)]
    d["norms"] = np.stack([np.concatenate(p) for p in norms])
    gains = np.zeros((DEPTH, 1024), f)
    for l in range(DEPTH):
        gains[l] = np.concatenate([np.tile(a["gqa_q_norm"][l], GQA_HEADS), np.tile(a["gqa_k_norm"][l], GQA_KV),
                                   a["mla_q_norm"][l], a["mla_kv_norm"][l]])
    d["head_gain"] = gains
    inside, dr, dc = _window_index()
    b = np.where(inside, a["na_rpb"][:, :, dr, dc], f(NEG)).astype(f)
    d["bias"] = np.ascontiguousarray(
        b.reshape(DEPTH, NA_HEADS, NT, P, T).transpose(0, 1, 3, 2, 4).reshape(DEPTH, NA_HEADS, P, NT * T))

    def each(name, widths, group):
        return np.stack([_packed(w, widths, group) for w in a[name]])
    d["w_in"] = each("w_in", Z_WIDTHS, KD)
    d["w_uq"] = each("mla_w_uq", [384], 2)
    d["w_ukv"] = each("mla_w_ukv", [512], 1)
    d["w_pa"] = each("w_proj_a", [1024], 2)
    d["w_pb"] = each("w_proj_b", [1024], 4)
    d["w_pc"] = each("w_proj_c", [1024], 2)
    d["w_out"] = each("w_out", [512] * 2, KD)
    d["mem_wq"] = each("mem_wq", [512] * 2, KD)
    d["mem_wkv"] = each("mem_wkv", [512] * 4, KD)
    d["mem_wo"] = each("mem_wo", [512] * 2, KD)
    d["ffn_up"], d["ffn_down"] = _experts(a["ffn_w_gu"], a["ffn_w_down"])
    d["moe_up"], d["moe_down"] = _experts(a["moe_w_gu"][0], a["moe_w_down"][0])
    d["router"] = a["moe_router"][0].reshape(KD, P, N_EXPERTS).transpose(1, 0, 2).reshape(P, -1)
    d["even_in"] = _packed(a["even_w_in_2"][0], [512] * 10, KD)
    d["even_out"] = _packed(a["even_w_out_2"][0], [512] * 2, 6)
    d["glu"] = _packed(a["ssm_glu_w_2"][0], [512], 4)
    d["odd_in"] = _packed(a["odd_w_in_2"][0], [512] * 8, KD)
    d["odd_out"] = _packed(a["odd_w_out_2"][0], [512] * 2, 8)
    d["pool_w"] = np.stack([_packed(w, [512], 4) for w in a["pool_w_2"][0]])
    par = [a["ssm_a_re_2"][0], a["ssm_a_im_2"][0], np.repeat(a["ssm_log_dt_2"][0][:, None], 64, axis=1)]
    d["ssm_par"] = np.stack([p.reshape(SSM_TILES, P)[TILE_AT].T for p in par], axis=1).reshape(P, -1)
    w = np.zeros((P, 2, 1024), f)
    for c, (bm, cm) in enumerate(((a["ssm_b_re_2"][0], a["ssm_c_re_2"][0]), (a["ssm_b_im_2"][0], a["ssm_c_im_2"][0]))):
        vb = w[:, 0].reshape(P, 2, 4, P)
        vc = w[:, 1].reshape(P, 2, SSM_TILES, 32)
        for g in range(32):
            j, half = g // 2, g % 2
            q0 = 32 * (j % 4) + 16 * half
            vb[q0:q0 + 16, c, j // 4, 64 * half:64 * half + 64] = bm[g].T
            vc[64 * half:64 * half + 64, c, TILE_AT.index(j), 16 * half:16 * half + 16] = cm[g].T
    d["ssm_w"] = w.reshape(P, -1)
    d["ssm_vec"] = np.concatenate([a["ssm_d_2"][0], a["ssm_glu_b_2"][0]])[None]
    d["pool_scale"] = a["pool_scale_2"]
    return {k: np.ascontiguousarray(v) for k, v in d.items()}


def kernel(**inputs):
    import concourse.bacc as bacc
    from concourse.bass_utils import run_bass_kernel_spmd
    arrays = _layout(inputs)
    nc = bacc.Bacc("TRN2", target_bir_lowering=False, num_devices=1)
    d = {k: nc.dram_tensor(f"in_{k}", v.shape, F32, kind="ExternalInput").ap() for k, v in arrays.items()}
    out = nc.dram_tensor("out", (1, T, D), F32, kind="ExternalOutput").ap()
    program(nc, d, out)
    r = run_bass_kernel_spmd(nc, [{f"in_{k}": v for k, v in arrays.items()}], core_ids=[0])
    return r.results[0]["out"]
```

```python
from contextlib import ExitStack, contextmanager

import numpy as np

import concourse.bass as bass
from concourse import mybir

ALU = mybir.AluOpType
ACT = mybir.ActivationFunctionType
F32 = mybir.dt.float32
U32 = mybir.dt.uint32
AX = mybir.AxisListType

P = 128
T = 256
NT = T // P
D = 1024
KD = D // P
DEPTH = 2
GRID_W = 64
HD = 64
ROPE_THETA = 10000.0
LN_EPS = 1e-5
RMS_EPS = 1e-6
NA_HEADS, NA_COLS = 4, 16
GQA_HEADS, GQA_KV = 8, 2
MLA_HEADS, NOPE, ROPE_C, MLA_V = 4, 64, 32, 64
DQ, DKV = 256, 128
MEM_HEADS, MEM_HD = 4, 256
D_FF = ((8 * D // 3 + 127) // 128) * 128
KF = D_FF // P
N_EXPERTS = 8
ALPHA = (2 * DEPTH) ** 0.25
A_Q, A_K, A_V = 0, 256, 512
B_Q, B_K, B_V = 768, 1280, 1408
C_DQ, C_DKV, C_KR = 1536, 1792, 1920
ZQ = 1952
ZIN = ZQ + 3 * D
Z_WIDTHS = [512, 512, 512, 416] + [512] * 6
ATT_HEADS = 16
ROT = 16
THETA_2 = 500000.0
SSM_W = 512
SSM_TILES = 16
E_Q, E_K, E_V, E_G, E_U, E_GS = 0, 1024, 2048, 3072, 4096, 4608
EVEN_IN, EVEN_OUT = 5120, 1536
POOL_W = 2048
POOL_WINDOWS = (2, 4, 8, 16)
NEG = -1.0e30
TWO_PI_HI = 6.28125
TWO_PI_LO = 2 * np.pi - TWO_PI_HI
TURN = 6.2831845
ROUND = 1.5 * 2.0 ** 23
TWO_PI = 2 * np.pi

SLOT = 5120
NSLOT = 4
HID_CHUNKS = D_FF // 256
DOWN_GROUPS = [5, 5, 4, 4, 4]
C_ID, C_COSB, C_SINB, C_COSC, C_SINC, C_COS2, C_SIN2, C_DMASK, C_DMUL = 0, 128, 192, 256, 288, 320, 336, 352, 864
C_TIME, C_IOTA8 = 1376, 1632
C_UPPER, C_ONES = 1640, 1768
C_END = 1896


TILE_AT = [(m // 2) % 4 + 4 * (2 * (m // 8) + m % 2) for m in range(SSM_TILES)]


def weight_tiles(k_tiles, widths, group):
    off, out = 0, []
    for c, w in enumerate(widths):
        k = 0
        while k < k_tiles:
            n = min(group, k_tiles - k)
            out.append((c, k, n, w, off))
            off += n * w
            k += n
    return out


class Line:

    def __init__(self, eng, sems):
        self.eng, self.sems = eng, sems
        self.seen, self.reg, self.per = {}, None, {}

    def value(self, name, count):
        if self.reg is not None and self.per.get(name):
            return self.reg * self.per[name] + count
        return count

    def at(self, name, count):
        return self.sems(name), self.value(name, count)

    def next(self, name, k=1):
        self.seen[name] = self.seen.get(name, 0) + k
        return self.at(name, self.seen[name])

    def passed(self, name, k=1):
        self.seen[name] = self.seen.get(name, 0) + k

    @contextmanager
    def loop(self, n, per):
        before = dict(self.seen)
        self.per = per
        with self.eng.Fori(0, n) as reg:
            self.reg = reg
            yield reg
            self.reg = None
        for k, v in self.seen.items():
            d = v - before.get(k, 0)
            if d:
                assert per.get(k, 0) == d, (k, d, per.get(k))
                self.seen[k] += (n - 1) * d


class Banks:

    def __init__(self, name, n, views):
        self.name, self.n, self.views = name, n, views
        self.next, self.uses = 0, [0] * n
        self.order = list(range(n))

    def emptied(self, b):
        return f"{self.name}{b}_emptied"


def program(nc, d, out, stop=None):
    ctx = ExitStack()
    with ctx:
        def sb(name, shape, dt=F32):
            return ctx.enter_context(nc.sbuf_tensor(name, shape, dt))

        sem_table = {}

        def sems(name):
            if name not in sem_table:
                sem_table[name] = ctx.enter_context(nc.semaphore(name))
            return sem_table[name]

        weights = sb("weights", [P, NSLOT, SLOT])
        h = sb("h", [P, NT, D])
        hT = sb("hT", [P, KD, T])
        big_flat = sb("big", [P, NT * EVEN_IN])
        att = sb("att", [P, 6144])
        prob = sb("prob", [P, 2, NT, T])
        probT = sb("probT", [P, 2, NT, T])
        bias = sb("bias", [P, 2, NT, T])
        norm_par = sb("norm_par", [P, 2, 2, D])
        head_gain = sb("head_gain", [P, 1024])
        const = sb("const", [P, C_END])
        k_rope = sb("k_rope", [P, NT, ROPE_C])
        stats = sb("stats", [P, NT, 2, 6])
        mv = sb("mv", [P, NT, 2])
        rstd = sb("rstd", [P, NT, 16])
        smax = sb("smax", [P, 2, NT])
        rsum = sb("rsum", [P, 2, NT])
        ssum = sb("ssum", [P, 2, NT])
        router_w = sb("router_w", [P, KD, N_EXPERTS])
        logit = sb("logit", [P, NT, N_EXPERTS])
        top = sb("top", [P, NT, 8])
        top_i = sb("top_i", [P, NT, 8], U32)
        top_f = sb("top_f", [P, NT, 8])
        gate = sb("gate", [P, NT, N_EXPERTS + 1])
        tmp8 = sb("tmp8", [P, NT, N_EXPERTS])
        chosen = sb("chosen", [P, NT, N_EXPERTS])
        place = sb("place", [P, NT, N_EXPERTS + 1])
        most = sb("most", [P, 1])
        bias_values = sb("bias_values", [P, 2])
        most_i = sb("most_i", [P, 1], mybir.dt.int32)
        ssm_par = sb("ssm_par", [P, 3, SSM_TILES])
        ssm_s = sb("ssm_s", [P, 16, SSM_TILES])

        headT = att[:, 0:4096]
        yT = att[:, 4096:6144].rearrange("p (k t) -> p k t", t=T)
        big = big_flat[:, 0:NT * ZIN].rearrange("p (t n) -> p t n", t=NT)
        wide = big_flat[:, :].rearrange("p (t n) -> p t n", t=NT)
        ident = const[:, C_ID:C_ID + P]

        hidT = big_flat[:, 0:KF * T].rearrange("p (k t) -> p k t", t=T)
        hid = big_flat[:, KF * T:KF * T + 1024].rearrange("p (b t n) -> p b t n", b=2, t=NT)
        silu = att[:, 0:1024].rearrange("p (b t n) -> p b t n", b=2, t=NT)
        hidT_few = big_flat[:, 0:KF * P].rearrange("p (k t) -> p k t", t=P)
        h_rows = att[:, 1024:3072].rearrange("p (t n) -> p t n", t=NT)
        few_T = att[:, 3072:4096].rearrange("p (k t) -> p k t", t=P)
        few_y = att[:, 4096:5120]
        pick = att[:, 5120:5376].rearrange("p (t n) -> p t n", t=NT)
        pick_gated = att[:, 5376:5632].rearrange("p (t n) -> p t n", t=NT)
        put_T = att[:, 5632:5888]
        hv = headT.rearrange("p (n t) -> p n t", t=T)
        mergedA = att[:, 0:2048].rearrange("p (t n) -> p t n", t=NT)
        ssm_b = att[:, 2048:3072].rearrange("p (c j n) -> p c j n", c=2, j=4)
        ssm_c = att[:, 3072:4096].rearrange("p (c j n) -> p c j n", c=2, j=SSM_TILES)
        ssm_vec = att[:, 4096:5120].rearrange("p (c n) -> p c n", c=2)
        sinT = big_flat[:, 0:1024].rearrange("p (b i t) -> p b i t", b=2, i=2)
        cosT = big_flat[:, 1024:2048].rearrange("p (b i t) -> p b i t", b=2, i=2)
        rot_in = big_flat[:, 2048:3072].rearrange("p (c i t) -> p c i t", c=2, i=2)
        at1 = EVEN_IN
        tmpA = big_flat[:, at1:at1 + 512].rearrange("p (i t) -> p i t", i=2)
        tmpB = big_flat[:, at1 + 512:at1 + 1024].rearrange("p (i t) -> p i t", i=2)
        scanned = big_flat[:, at1 + 1024:at1 + 2048].rearrange("p (c i t) -> p c i t", c=2, i=2)
        ssm_state = big_flat[:, at1 + 2048:at1 + 3072].rearrange("p (c i t) -> p c i t", c=2, i=2)
        window = att[:, 4096:6144].rearrange("p (g s t) -> p g s t", g=4, s=NT)
        pool_scale = big_flat[:, 8192:10240]
        y_out = big_flat[:, 0:2048].rearrange("p (t n) -> p t n", t=NT)

        ssm_v = [ssm_s[:, i, :] for i in range(16)]
        pool_tmp = [att[:, a:a + 512].rearrange("p (i t) -> p i t", i=2) for a in (512, 1536)]

        def e(t, col, n):
            return wide[:, t, col:col + n]

        even_merged_parts = [buf.rearrange("p b t n -> p (b t) n") for buf in (prob, probT, bias)]

        def even_merged_T(k, t):
            return even_merged_parts[k // 4][:, k % 4, t * P:(t + 1) * P]

        def head_tiles(g):
            q, k = [(att[:, 0:1024], att[:, 1024:2048]),
                    (att[:, 5120:6144], bias[:, :, :, :].rearrange("p b t n -> p (b t n)"))][g % 2]
            return [buf.rearrange("p (n t) -> p n t", t=T) for buf in (q, k)]

        def groups_next(i):
            g, at = i // 4 + 1, i % 4
            return [(g, 4 * at), (g, 4 * at + 2)] if g < ATT_HEADS // 4 and at < 2 else []

        def table(col, n):
            return const[:, col:col + NT * n].rearrange("p (t n) -> p t n", t=NT)

        pair_mem = [ctx.enter_context(nc.psum_tensor(f"pair{i}", [P, NT, 512], F32)) for i in range(2)]
        bank_mem = [ctx.enter_context(nc.psum_tensor(f"bank{i}", [P, 512], F32)) for i in range(4)]
        pairs = Banks("pair", 2, pair_mem)
        banks = Banks("bank", 4, bank_mem)
        jobs, tiles_used = {}, [0]
        ended_in = {}

        block = ctx.enter_context(nc.Block())
        STAGES = ["emb", "mix0", "mem0", "ffn0", "mix1", "mem1", "ffn1", "even", "odd"]
        n_stages = len(STAGES) if stop is None else STAGES.index(stop) + 1

        def on(stage):
            return STAGES.index(stage) < n_stages

        PER_EXPERT = {"banks_filled": HID_CHUNKS * 2 + 2, "pair0_emptied": 7, "pair1_emptied": 6,
                      "bank0_emptied": 3, "bank1_emptied": 3, "bank2_emptied": 3, "bank3_emptied": 2,
                      "silu_done": HID_CHUNKS}
        for s in range(NSLOT):
            PER_EXPERT[f"slot{s}_landed"] = 16 * 4
            PER_EXPERT[f"slot{s}_used"] = 4
        PER_FEW = dict(PER_EXPERT, banks_filled=HID_CHUNKS * 2 + 7, pair0_emptied=8, pair1_emptied=7,
                       bank0_emptied=4, bank1_emptied=4, bank2_emptied=3, bank3_emptied=3, picks_ready=1)
        surplus = {}

        @block.tensor
        def _(pe):
            L = Line(pe, sems)
            filled = [0]
            slot_owed = [None]
            filling = [None]

            def mm(o, lhsT, rhs, **flags):
                ins = pe.matmul(o, lhsT, rhs, **flags)
                if slot_owed[0] is not None:
                    ins.then_inc(sems(slot_owed[0]), 1)
                    slot_owed[0] = None
                return ins

            def mm_t(o, src, identity):
                return mm(o, src, identity, is_transpose=True, start=True, stop=True)

            def begin(ring, name, late=False, b=None):
                if b is None:
                    b = ring.order[ring.next % len(ring.order)]
                    ring.next += 1
                if ring.uses[b]:
                    pe.wait_ge(*L.at(ring.emptied(b), ring.uses[b]))
                ring.uses[b] += 1
                if not late:
                    filled[0] += 1
                jobs[name] = (ring, b, filled[0], ring.uses[b])
                return ring.views[b]

            def end_late(ins, name):
                ring, b, _, use = jobs[name]
                filled[0] += 1
                jobs[name] = (ring, b, filled[0], use)
                end(ins)

            def end(ins):
                ins.then_inc(sems("banks_filled"), 1)

            def emptied(name):
                ring, b, _, use = jobs[name]
                return L.at(ring.emptied(b), use)

            def transpose_rows(name, src, k_tiles):
                for j in range(0, k_tiles, 2):
                    o = begin(banks, (name, j))
                    n = min(2, k_tiles - j)
                    for i in range(n):
                        for t in range(NT):
                            ins = mm_t(o[:, (i * NT + t) * P:(i * NT + t + 1) * P], src(t, j + i), ident)
                    end(ins)

            def next_tile():
                n = tiles_used[0]
                tiles_used[0] += 1
                s = n % NSLOT
                pe.wait_ge(*L.at(f"slot{s}_landed", 16 * (n // NSLOT + 1)))
                return s

            def product(name, lhsT, k_tiles, widths, group):
                tiles = weight_tiles(k_tiles, widths, group)
                outs = []
                for c, k0, nk, w, _ in tiles:
                    s = next_tile()
                    n_out = -(-w // 512)
                    if k0 == 0:
                        outs = [begin(pairs, (name, c * n_out + i)) for i in range(n_out)]
                    for i, o in enumerate(outs):
                        n = min(512, w - 512 * i)
                        for t in range(NT):
                            for k in range(nk):
                                at = k * w + 512 * i
                                ins = mm(o[:, t, 0:n], lhsT(k0 + k, t), weights[:, s, at:at + n],
                                                start=(k0 + k == 0), stop=(k0 + k == k_tiles - 1))
                        if k0 + nk == k_tiles:
                            end(ins)
                    if k0 + nk == k_tiles:
                        slot_owed[0] = f"slot{s}_used"
                    else:
                        ins.then_inc(sems(f"slot{s}_used"), 1)

            def product_in_steps(name, lhsT, k_tiles, widths, per_step, copied=True):
                n = 0
                for c, k0, nk, w, _ in weight_tiles(k_tiles, widths, k_tiles):
                    s = next_tile()
                    o = begin(pairs, (name, c), late=True)
                    for t in range(NT):
                        for k in range(nk):
                            ins = mm(o[:, t, 0:w], lhsT(k, t), weights[:, s, k * w:k * w + w],
                                     start=(k == 0), stop=(k == nk - 1))
                            n += 1
                            if (t, k) == (NT - 1, nk - 1):
                                end_late(ins, (name, c))
                                slot_owed[0] = f"slot{s}_used"
                                if copied:
                                    ended_in.setdefault(filling[0], []).append((name, c))
                            if n % per_step == 0:
                                yield

            def partial_product(outs, lhsT, nk, start, name=None):
                s = next_tile()
                for t in range(NT):
                    for k in range(nk):
                        ins = mm(outs[t], lhsT(k, t), weights[:, s, 512 * k:512 * k + 512],
                                 start=(start and k == 0), stop=(name is not None and k == nk - 1),
                                 skip_group_check=True)
                        if name is None and (t, k) == (NT - 1, nk - 1):
                            ins.then_inc(sems(f"slot{s}_used"), 1)
                        elif name is not None and k == nk - 1 and (t == NT - 1 or name[t] != name[t + 1]):
                            end_late(ins, name[t])
                            if t == NT - 1:
                                slot_owed[0] = f"slot{s}_used"
                        yield

            def tiles_used_at(s):
                return (tiles_used[0] - 1) // NSLOT + 1

            def hT_at(k, t):
                return hT[:, k, t * P:(t + 1) * P]

            def yT_at(k, t):
                return yT[:, k, t * P:(t + 1) * P]

            def heads(name, specs, filler=iter(()), steps=2, before=lambda i: None, behind=lambda i: None):
                n = len(specs)
                for i in range(n + 2):
                    filling[0] = (name, min(i, n - 1))
                    before(i)
                    if i < n:
                        qk, v, width, natural = specs[i]
                        o = begin(banks, (name, "score", i))
                        for t in range(NT):
                            for j, (q, k) in enumerate(qk):
                                ins = mm(o[:, t * T:(t + 1) * T], q[:, t * P:(t + 1) * P], k,
                                                start=(j == 0), stop=(j == len(qk) - 1))
                        end(ins)
                    for _ in range(steps):
                        next(filler, None)
                    if 1 <= i <= n:
                        m = i - 1
                        pe.wait_ge(*L.next("prob_ready"))
                        o = begin(banks, (name, "probT", m))
                        for j in range(NT):
                            for t in range(NT):
                                at = (j * NT + t) * P
                                ins = mm_t(o[:, at:at + P], prob[:, m % 2, t, j * P:(j + 1) * P], ident)
                        end(ins)
                    if i >= 2:
                        m = i - 2
                        qk, v, width, natural = specs[m]
                        pe.wait_ge(*emptied((name, "probT", m)))
                        o = begin(banks, (name, "value", m))
                        if natural:
                            for t in range(NT):
                                for j in range(NT):
                                    ins = mm(o[:, t * width:(t + 1) * width],
                                                    probT[:, m % 2, j, t * P:(t + 1) * P], v(j),
                                                    start=(j == 0), stop=(j == NT - 1))
                        else:
                            for c in range(-(-width // P)):
                                w = min(P, width - c * P)
                                for j in range(NT):
                                    ins = mm(o[0:w, c * T:(c + 1) * T], v(j)[:, c * P:c * P + w],
                                                    probT[:, m % 2, j, :], start=(j == 0), stop=(j == NT - 1))
                        end(ins)
                    behind(i)

            def head_transposes(name, srcs):
                for j in range(0, len(srcs), 2):
                    o = begin(banks, (name, j))
                    for i, src in enumerate(srcs[j:j + 2]):
                        for t in range(NT):
                            ap = src(t)
                            w = ap.shape[1]
                            at = (i * NT + t) * P
                            ins = mm_t(o[0:w, at:at + P], ap, ident)
                    end(ins)

            def hd(base, n, w=HD):
                return [lambda t, i=i: big[:, t, base + i * w:base + (i + 1) * w] for i in range(n)]

            pe.wait_ge(*L.next("const_landed", 16))

            def mixer(l):
                pe.wait_ge(*L.next("normed"))
                transpose_rows(("hT", "mix", l), lambda t, k: h[:, t, k * P:(k + 1) * P], KD)
                pe.wait_ge(*emptied((("hT", "mix", l), KD - 2)))
                product(("z", l), hT_at, KD, Z_WIDTHS[:4], KD)
                gates = product_in_steps(("g", l), hT_at, KD, Z_WIDTHS[4:], 2)
                pe.wait_ge(*emptied((("z", l), 0)))
                pe.wait_ge(*emptied((("z", l), 1)))
                head_transposes(("aT", l), hd(A_Q, 4) + hd(A_K, 4))
                filling[0] = ("ahead", l)
                for _ in range(NT * KD * 2 // 2):
                    next(gates)
                pe.wait_ge(*emptied((("aT", l), 4)))
                pe.wait_ge(*emptied((("aT", l), 6)))
                heads(("a", l), [([(hv[0:HD, i, :], hv[0:HD, 4 + i, :])],
                                  lambda j, i=i: big[:, j, A_V + i * HD:A_V + (i + 1) * HD], HD, False)
                                 for i in range(NA_HEADS)], gates)
                pe.wait_ge(*L.next("b_rotated", 2))
                head_transposes(("bT", l), hd(B_Q, 10))
                pe.wait_ge(*emptied((("bT", l), 6)))
                pe.wait_ge(*emptied((("bT", l), 8)))
                heads(("b", l), [([(hv[0:HD, i, :], hv[0:HD, 8 + i // 4, :])],
                                  lambda j, i=i: big[:, j, B_V + i // 4 * HD:B_V + (i // 4 + 1) * HD], HD, False)
                                 for i in range(GQA_HEADS)], gates)
                for _ in gates:
                    pass
                pe.wait_ge(*L.next("c_normed"))
                transpose_rows(("cT", l), lambda t, k: big[:, t, C_DQ + k * P:C_DQ + (k + 1) * P], 3)
                pe.wait_ge(*emptied((("cT", l), 2)))
                product(("uq", l), hT_at, 2, [384], 2)
                product(("ukv", l), lambda k, t: hT_at(2, t), 1, [512], 1)
                pe.wait_ge(*L.next("c_rotated", 2))
                head_transposes(("cqT", l), hd(0, 4, 96))
                head_transposes(("ckT", l),
                                [lambda t, i=i: big[:, t, B_Q + i * 128:B_Q + i * 128 + NOPE] for i in range(4)])
                head_transposes(("krT", l), [lambda t: k_rope[:, t, :]])
                pe.wait_ge(*emptied((("krT", l), 0)))
                pe.wait_ge(*emptied((("cqT", l), 2)))
                pa = product_in_steps(("pa", l), yT_at, 2, [512] * 2, 1, copied=False)
                heads(("c", l), [([(hv[0:96, i, :], hv[0:96, 4 + i, :])],
                                  lambda j, i=i: big[:, j, B_Q + i * 128 + NOPE:B_Q + (i + 1) * 128], MLA_V, False)
                                 for i in range(MLA_HEADS)], pa)
                for _ in pa:
                    pass
                product(("pb", l), lambda k, t: yT_at(2 + k, t), 4, [1024], 4)
                pe.wait_ge(*emptied((("c", l), "value", 3)))
                product(("pc", l), lambda k, t: yT_at(6 + k, t), 2, [1024], 2)
                pe.wait_ge(*L.next("merged"))
                transpose_rows(("mT", l), lambda t, k: mergedA[:, t, k * P:(k + 1) * P], KD)
                pe.wait_ge(*emptied((("mT", l), KD - 2)))
                product(("o", l), hT_at, KD, [512] * 2, KD)

            def cross(l):
                memory = big_flat[:, 0:2048].rearrange("p (t n) -> p t n", t=NT)
                memT = big_flat[:, 2048:4096].rearrange("p (k t) -> p k t", t=T)
                q = big_flat[:, 4096:6144].rearrange("p (t n) -> p t n", t=NT)
                k = big_flat[:, 6144:8192].rearrange("p (t n) -> p t n", t=NT)
                pe.wait_ge(*L.next("mem_landed", 16))
                transpose_rows(("memT", l), lambda t, kk: memory[:, t, kk * P:(kk + 1) * P], KD)
                pe.wait_ge(*emptied((("memT", l), KD - 2)))
                memT_at = lambda kk, t: memT[:, kk, t * P:(t + 1) * P]
                product(("kv", l), memT_at, KD, [512] * 3, KD)
                pe.wait_ge(*L.next("normed"))
                transpose_rows(("hT", "mem", l), lambda t, kk: h[:, t, kk * P:(kk + 1) * P], KD)
                transpose_rows(("xkT", l), lambda t, kk: k[:, t, kk * P:(kk + 1) * P], KD)
                pe.wait_ge(*emptied((("hT", "mem", l), KD - 2)))
                product(("q", l), hT_at, KD, [512] * 2, KD)
                pe.wait_ge(*emptied((("q", l), 1)))
                transpose_rows(("xqT", l), lambda t, kk: q[:, t, kk * P:(kk + 1) * P], KD)
                pe.wait_ge(*emptied((("xqT", l), KD - 2)))
                last_v = product_in_steps(("v", l), memT_at, KD, [512], 2)

                def values(i):
                    def v(j):
                        if (i, j) == (MEM_HEADS // 2, 0):
                            pe.wait_ge(*emptied((("v", l), 0)))
                        return memory[:, j, i * MEM_HD:(i + 1) * MEM_HD]
                    return v
                heads(("x", l), [([(hv[:, 2 * i + j, :], hv[:, 8 + 2 * i + j, :]) for j in range(2)],
                                  values(i), MEM_HD, False) for i in range(MEM_HEADS)], last_v)
                pe.wait_ge(*emptied((("x", l), "value", 3)))
                product(("xo", l), yT_at, KD, [512] * 2, KD)

            def ffn_body(name):
                for c in range(HID_CHUNKS + 1):
                    if c < HID_CHUNKS:
                        s = next_tile()
                        o = begin(pairs, (name, "up", c))
                        for t in range(NT):
                            for k in range(KD):
                                ins = mm(o[:, t, :], hT_at(k, t), weights[:, s, k * 512:(k + 1) * 512],
                                                start=(k == 0), stop=(k == KD - 1))
                        end(ins)
                        slot_owed[0] = f"slot{s}_used"
                    if c:
                        pe.wait_ge(*emptied((name, "up", c - 1)))
                        o = begin(banks, (name, "hidT", c - 1))
                        for i in range(2):
                            for t in range(NT):
                                at = (i * NT + t) * P
                                ins = mm_t(o[:, at:at + P], hid[:, (c - 1) % 2, t, i * P:(i + 1) * P], ident)
                        end(ins)
                pe.wait_ge(*emptied((name, "hidT", HID_CHUNKS - 1)))
                pe.wait_ge(*emptied((name, "hidT", HID_CHUNKS - 2)))
                outs = [begin(pairs, (name, "down", i)) for i in range(2)]
                k0 = 0
                for g, nk in enumerate(DOWN_GROUPS):
                    s = next_tile()
                    for i in range(2):
                        for t in range(NT):
                            for k in range(nk):
                                at = k * 1024 + 512 * i
                                ins = mm(outs[i][:, t, :], hidT[:, k0 + k, t * P:(t + 1) * P],
                                                weights[:, s, at:at + 512],
                                                start=(k0 + k == 0), stop=(k0 + k == KF - 1))
                        if g == len(DOWN_GROUPS) - 1 and i == 0:
                            end(ins)
                    ins.then_inc(sems(f"slot{s}_used"), 1)
                    k0 += nk
                pe.wait_ge(*L.at(f"slot{s}_used", tiles_used_at(s)))
                pe.sem_inc(sems("banks_filled"), 1)

            def gather_few(name):
                for g in range(2):
                    o = begin(banks, (name, g))
                    for kk in range(4):
                        k = 4 * g + kk
                        for t in range(NT):
                            ins = mm(o[:, kk * P:(kk + 1) * P], h_rows[:, t, k * P:(k + 1) * P], pick[:, t, :],
                                     start=(t == 0), stop=(t == NT - 1))
                    end(ins)

            def few_body():
                o = begin(banks, ("few", "put"))
                for t in range(NT):
                    ins = mm_t(o[:, t * P:(t + 1) * P], pick_gated[:, t, :], ident)
                end(ins)
                pe.wait_ge(*emptied(("few_gather", 0)))
                pe.wait_ge(*emptied(("few_gather", 1)))
                for c in range(HID_CHUNKS + 1):
                    if c < HID_CHUNKS:
                        s = next_tile()
                        o = begin(pairs, ("few", "up", c))
                        for k in range(KD):
                            ins = mm(o[:, 0, :], few_T[:, k, :], weights[:, s, k * 512:(k + 1) * 512],
                                     start=(k == 0), stop=(k == KD - 1))
                        end(ins)
                        slot_owed[0] = f"slot{s}_used"
                    if c:
                        pe.wait_ge(*emptied(("few", "up", c - 1)))
                        o = begin(banks, ("few", "hidT", c - 1))
                        for i in range(2):
                            ins = mm_t(o[:, i * P:(i + 1) * P], hid[:, (c - 1) % 2, 0, i * P:(i + 1) * P], ident)
                        end(ins)
                pe.wait_ge(*emptied(("few", "hidT", HID_CHUNKS - 1)))
                pe.wait_ge(*emptied(("few", "hidT", HID_CHUNKS - 2)))
                outs = [begin(pairs, ("few", "down", i)) for i in range(2)]
                k0 = 0
                for g, nk in enumerate(DOWN_GROUPS):
                    s = next_tile()
                    for i in range(2):
                        for k in range(nk):
                            at = k * 1024 + 512 * i
                            ins = mm(outs[i][:, 0, :], hidT_few[:, k0 + k, :], weights[:, s, at:at + 512],
                                     start=(k0 + k == 0), stop=(k0 + k == KF - 1))
                        if g == len(DOWN_GROUPS) - 1:
                            end(ins)
                    if g < len(DOWN_GROUPS) - 1:
                        ins.then_inc(sems(f"slot{s}_used"), 1)
                    k0 += nk
                slot_owed[0] = f"slot{s}_used"
                pe.wait_ge(*L.next("picks_ready"))
                gather_few("few_gather_next")
                pe.wait_ge(*emptied(("few", "put")))
                for i in range(2):
                    pe.wait_ge(*emptied(("few", "down", i)))
                    o = begin(pairs, ("few", "sum", i))
                    for t in range(NT):
                        ins = mm(o[:, t, :], put_T[:, t * P:(t + 1) * P], few_y[:, 512 * i:512 * i + 512],
                                 start=True, stop=True)
                    end(ins)

            def loop_experts(n, per, body):
                before = (filled[0], list(pairs.uses), list(banks.uses), tiles_used[0])
                pairs.next = banks.next = 0
                with L.loop(n, per):
                    body()
                assert filled[0] - before[0] == per["banks_filled"]
                more = n - 1
                filled[0] += more * (filled[0] - before[0])
                for ring, b in ((pairs, before[1]), (banks, before[2])):
                    for i in range(ring.n):
                        step = ring.uses[i] - b[i]
                        assert per[ring.emptied(i)] == step, (ring.name, i, step)
                        ring.uses[i] += more * step
                tiles_used[0] += more * (tiles_used[0] - before[3])
                pairs.next = banks.next = 0

            def counts():
                c = {"banks_filled": filled[0]}
                for ring in (pairs, banks):
                    c.update({ring.emptied(i): ring.uses[i] for i in range(ring.n)})
                return c

            def moe():
                pe.wait_ge(*L.next("chosen_ready"))
                upper, ones = const[:, C_UPPER:C_UPPER + P], const[:, C_ONES:C_ONES + P]
                o = begin(banks, ("places",))
                mm(o[:, 0:8], upper, chosen[:, 0, :], start=True, stop=True)
                mm(o[:, 8:16], ones, chosen[:, 0, :], start=True, stop=False)
                mm(o[:, 8:16], upper, chosen[:, 1, :], start=False, stop=True)
                mm(o[:, 16:24], ones, chosen[:, 0, :], start=True, stop=False)
                end(mm(o[:, 16:24], ones, chosen[:, 1, :], start=False, stop=True))
                pe.wait_ge(*L.next("count_ready"))
                largest = pe.value_load(most_i[0:1, 0:1], min_val=0, max_val=T)
                start = (counts(), list(pairs.uses), list(banks.uses), tiles_used[0], dict(L.seen))
                with pe.If(largest < P + 1):
                    pairs.next = banks.next = 0
                    pe.wait_ge(*L.next("picks_ready"))
                    gather_few("few_gather")
                    loop_experts(N_EXPERTS, PER_FEW, few_body)
                few = (counts(), list(pairs.uses), list(banks.uses), dict(L.seen))
                filled[0] = start[0]["banks_filled"]
                pairs.uses, banks.uses, tiles_used[0], L.seen = start[1], start[2], start[3], start[4]
                with pe.Else():
                    loop_experts(N_EXPERTS, PER_EXPERT, lambda: ffn_body(("ffn", 1)))
                    surplus.update({k: few[0][k] - v for k, v in counts().items()})
                    for i in range(2):
                        ring, b, _, _ = jobs[("ffn", 1), "down", i]
                        pe.wait_ge(*L.at(ring.emptied(b), ring.uses[b]))
                    pe.sem_inc(sems("banks_filled"), surplus["banks_filled"])
                filled[0], pairs.uses, banks.uses, L.seen = few[0]["banks_filled"], few[1], few[2], few[3]

            def ffn(l):
                pe.wait_ge(*L.next("normed"))
                transpose_rows(("hT", "ffn", l), lambda t, k: h[:, t, k * P:(k + 1) * P], KD)
                if l == 1:
                    pe.wait_ge(*L.next("router_landed", 16))
                pe.wait_ge(*emptied((("hT", "ffn", l), KD - 2)))
                if l == 0:
                    ffn_body(("ffn", 0))
                else:
                    o = begin(banks, ("router", l))
                    for t in range(NT):
                        for k in range(KD):
                            ins = mm(o[:, t * 8:t * 8 + 8], hT_at(k, t), router_w[:, k, :],
                                     start=(k == 0), stop=(k == KD - 1))
                    end(ins)
                    moe()

            def even():
                pe.wait_ge(*L.next("normed", 2))
                xn = att[:, 0:2048].rearrange("p (t n) -> p t n", t=NT)
                transpose_rows(("eT",), lambda t, k: xn[:, t, k * P:(k + 1) * P], KD)
                pe.wait_ge(*emptied((("eT",), KD - 2)))
                product(("ez",), hT_at, KD, [512] * 6, KD)
                rest = product_in_steps(("er",), hT_at, KD, [512] * 4, 1)
                filling[0] = "ahead of even's heads"
                for _ in range(4):
                    next(rest)
                pe.wait_ge(*L.next("e_rotated", 2))

                def transposes(g, j):
                    base = (E_Q if j < 4 else E_K) + (4 * g + j % 4) * HD
                    head_transposes(("ehT", g, j), [lambda t, i=i: e(t, base + i * HD, HD) for i in range(2)])

                def before(i):
                    if i % 4 == 0 and i < ATT_HEADS:
                        for j in range(0, 8, 2):
                            pe.wait_ge(*emptied((("ehT", i // 4, j), 0)))

                def behind(i):
                    for g, j in groups_next(i):
                        transposes(g, j)

                def spec(i):
                    q, k = head_tiles(i // 4)
                    return ([(q[0:HD, i % 4, :], k[0:HD, i % 4, :])], lambda j: e(j, E_V + i * HD, HD), HD, True)
                for j in range(0, 8, 2):
                    transposes(0, j)
                heads("e", [spec(i) for i in range(ATT_HEADS)], rest, 3, before, behind)
                filling[0] = "behind even's heads"
                for _ in rest:
                    pass
                pe.wait_ge(*emptied((("er",), 2)))
                transpose_rows(("uT",), lambda t, k: e(t, E_U + k * P, P), 4)
                uT = hT
                pe.wait_ge(*emptied((("uT",), 2)))
                pe.wait_ge(*L.next("ssm_w_landed", 16))
                y = begin(pairs, ("ssm_y",), late=True)
                em = even_merged_T
                outs, names = [], []
                eo = begin(pairs, (("eo",), 0), late=True)
                outs.append([eo[:, t, :] for t in range(NT)])
                names.append([(("eo",), 0)] * NT)
                names.append([(("eo", 1), t) for t in range(NT)])

                def attention_part():
                    outs.append([begin(banks, names[1][t], late=True, b=2 + t)[:, :] for t in range(NT)])
                    for c in range(2):
                        yield from partial_product(outs[c], lambda k, t: em(k, t), KD, True)

                def fill(n):
                    for _ in range(n):
                        next(rest, None)

                rest = attention_part()
                banks.order = [0, 1]
                for b in range(SSM_TILES // 2 + 1):
                    if b < SSM_TILES // 2:
                        for part in range(2):
                            o = begin(banks, ("Bu", b, part))
                            for i in range(2):
                                j = TILE_AT[2 * b + i]
                                q0 = 32 * (j % 4)
                                ins = mm(o[:, i * T:(i + 1) * T],
                                                ssm_b[q0:q0 + 32, part, j // 4, :],
                                                uT[q0:q0 + 32, j // 4, :], start=True, stop=True,
                                                tile_position=(q0, 0))
                            end(ins)
                    if b == 0:
                        pe.wait_ge(*L.next("ssm_space"))
                    if b < 2:
                        for j in (4 * b, 4 * b + 2):
                            o = begin(banks, (("emT",), j), b=2 + j // 2 % 2)
                            for i in range(2):
                                for t in range(NT):
                                    ins = mm_t(o[:, (i * NT + t) * P:(i * NT + t + 1) * P],
                                               e(t, E_G + (j + i) * P, P), ident)
                            end(ins)
                    elif b == 2:
                        pe.wait_ge(*emptied((("emT",), 4)))
                        pe.wait_ge(*emptied((("emT",), 6)))
                    if 2 <= b < SSM_TILES // 2:
                        fill(1)
                    if b:
                        pe.wait_ge(*L.next("re_ready"))
                        pe.wait_ge(*L.next("im_ready"))
                        for i in range(2):
                            m = 2 * (b - 1) + i
                            j = TILE_AT[m]
                            for t in range(NT):
                                for part in range(2):
                                    ins = mm(y[:, t, 32 * j:32 * j + 32],
                                                    ssm_state[:, part, i, t * P:(t + 1) * P],
                                                    ssm_c[:, part, m, :], start=(part == 0), stop=(part == 1),
                                                    skip_group_check=True)
                        if b == SSM_TILES // 2:
                            end_late(ins, ("ssm_y",))
                        else:
                            ins.then_inc(sems("states_used"), 1)
                    if 2 <= b < SSM_TILES // 2:
                        fill(2)
                fill(4)
                pe.wait_ge(*L.next("gelu_done"))
                transpose_rows(("gT",), lambda t, k: e(t, E_U + k * P, P), 4)
                pe.wait_ge(*emptied((("gT",), 2)))
                product(("glu",), hT_at, 4, [512], 4)
                for _ in rest:
                    pass
                pe.wait_ge(*L.next("even_merged"))
                transpose_rows(("smT",), lambda t, k: e(t, E_U + k * P, P), 4)
                pe.wait_ge(*emptied((("smT",), 0)))
                pe.wait_ge(*emptied((("smT",), 2)))
                for c in range(2):
                    for _ in partial_product(outs[c], lambda k, t: em(KD + k, t), 4, False, names[c]):
                        pass
                banks.order = [0, 1, 2, 3]

            def odd():
                pe.wait_ge(*L.next("normed", 2))
                xn = att[:, 0:2048].rearrange("p (t n) -> p t n", t=NT)
                transpose_rows(("dT",), lambda t, k: xn[:, t, k * P:(k + 1) * P], KD)
                pe.wait_ge(*emptied((("dT",), KD - 2)))
                product(("dz",), hT_at, KD, [512] * 8, KD)
                u = big_flat[:, 0:4096].rearrange("p (t n) -> p t n", t=NT)
                g = big_flat[:, 4096:8192].rearrange("p (t n) -> p t n", t=NT)
                pe.wait_ge(*L.next("window_landed", 16))
                pe.wait_ge(*emptied((("dz",), 3)))
                mixT = att[:, 0:4096].rearrange("p (k t) -> p k t", t=T)
                for j in range(0, 16, 2):
                    o = begin(banks, ("mixT", j))
                    for i in range(2):
                        for s in range(NT):
                            ins = mm(o[:, i * T:(i + 1) * T], u[:, s, (j + i) * P:(j + i + 1) * P],
                                            window[:, j // 4, s, :], start=(s == 0), stop=(s == NT - 1))
                    end(ins)
                pe.wait_ge(*emptied(("mixT", 14)))
                for gi in range(4):
                    product(("pw", gi), lambda k, t: mixT[:, 4 * gi + k, t * P:(t + 1) * P], 4, [512], 4)
                pe.wait_ge(*L.next("odd_gated"))
                transpose_rows(("odT",), lambda t, k: g[:, t, k * P:(k + 1) * P], 16)
                pe.wait_ge(*emptied((("odT",), 14)))
                product(("do",), lambda k, t: mixT[:, k, t * P:(t + 1) * P], 16, [512] * 2, 8)

            for l in range(DEPTH):
                if on(f"mix{l}"):
                    mixer(l)
                if on(f"mem{l}"):
                    cross(l)
                if on(f"ffn{l}"):
                    ffn(l)
            if on("even"):
                even()
            if on("odd"):
                odd()

        def consumer(L):
            def filled(name):
                return L.at("banks_filled", jobs[name][2])

            def bank(name):
                ring, b, _, _ = jobs[name]
                return ring.views[b], sems(ring.emptied(b))

            def emptied(name):
                ring, b, _, use = jobs[name]
                return L.at(ring.emptied(b), use)
            return filled, bank, emptied

        def bc(ap, axis, shape):
            return ap.unsqueeze(axis).to_broadcast(shape)

        @block.vector
        def _(ve):
            L = Line(ve, sems)
            filled, bank, emptied = consumer(L)
            norms = [0]

            def link(ins):
                ins.then_inc(sems("vector_step"), 1)
                ve.wait_ge(*L.next("vector_step"))

            def copy(name, dst, src=lambda o: o[:, :, :]):
                ve.wait_ge(*filled(name))
                o, free = bank(name)
                ve.tensor_copy(dst, src(o)).then_inc(free, 1)

            def copies(name, dst, k_tiles):
                for j in range(0, k_tiles, 2):
                    n = min(2, k_tiles - j)
                    copy((name, j), dst[:, j:j + n, :],
                         lambda o: o[:, 0:n * T].rearrange("p (k t) -> p k t", t=T))

            def head_copies(name, first, rows, n):
                for j in range(0, n, 2):
                    copy((name, j), hv[0:rows, first + j:first + j + 2, :],
                         lambda o: o[0:rows, :].rearrange("p (k t) -> p k t", t=T))

            def half_stats(src, c):
                for t in range(NT):
                    ins = ve.bn_stats(stats[:, t, c, :], src[:, t, 512 * c:512 * c + 512])
                if c:
                    link(ins)

            def mean_and_variance():
                for t in range(NT):
                    ins = ve.bn_aggr(mv[:, t, :], stats[:, t, :, :])
                link(ins)

            def norm_slot():
                s = norms[0] % 2
                norms[0] += 1
                if norms[0] == 1:
                    ve.wait_ge(*L.next("first_norm_landed", 16))
                else:
                    ve.wait_ge(*L.next(f"norm_par{s}_landed", 16))
                return norm_par[:, s, 0, :], norm_par[:, s, 1, :]

            def begin_root(v, eps, scale=1.0, src=None):
                ve.tensor_scalar(v, v if src is None else src, scale, eps, ALU.mult, ALU.add)\
                  .then_inc(sems("variance_ready"), 1)

            def finish_root(v):
                ve.wait_ge(*L.next("root_ready"))
                link(ve.reciprocal(v, v))

            def inverse_root(v, eps, scale=1.0):
                begin_root(v, eps, scale)
                finish_root(v)

            def layer_norm():
                mean_and_variance()
                begin_root(rstd[:, :, 0], LN_EPS, src=mv[:, :, 1])
                g, b = norm_slot()
                for t in range(NT):
                    ins = ve.scalar_tensor_tensor(h[:, t, :], h[:, t, :], mv[:, t, 0:1], g, ALU.subtract, ALU.mult)
                link(ins)
                finish_root(rstd[:, :, 0])
                for t in range(NT):
                    ins = ve.scalar_tensor_tensor(h[:, t, :], h[:, t, :], rstd[:, t, 0:1], b, ALU.mult, ALU.add)
                ins.then_inc(sems("normed"), 1)
                ve.wait_ge(*L.next("normed"))

            def begin_rms():
                mean_and_variance()
                link(ve.tensor_tensor(rstd[:, :, 1], mv[:, :, 0], mv[:, :, 0], ALU.mult))
                link(ve.tensor_tensor(rstd[:, :, 1], rstd[:, :, 1], mv[:, :, 1], ALU.add))
                begin_root(rstd[:, :, 0], RMS_EPS, src=rstd[:, :, 1])

            def pre_norm():
                for c in range(2):
                    half_stats(h, c)
                begin_rms()
                g, _ = norm_slot()
                finish_root(rstd[:, :, 0])
                for t in range(NT):
                    ins = ve.scalar_tensor_tensor(mergedA[:, t, :], h[:, t, :], rstd[:, t, 0:1], g,
                                                  ALU.mult, ALU.mult)
                ins.then_inc(sems("normed"), 1)
                ve.wait_ge(*L.next("normed"))

            def post_norm():
                begin_rms()
                g, _ = norm_slot()
                link(ve.tensor_tensor(y_out, y_out, bc(g, 1, [P, NT, D]), ALU.mult))
                finish_root(rstd[:, :, 0])
                for t in range(NT):
                    ins = ve.scalar_tensor_tensor(h[:, t, :], y_out[:, t, :], rstd[:, t, 0:1], h[:, t, :],
                                                  ALU.mult, ALU.add)
                ins.then_inc(sems("normed"), 1)
                ve.wait_ge(*L.next("normed"))

            def residual(name):
                for c in range(2):
                    ve.wait_ge(*filled((name, c)))
                    o, free = bank((name, c))
                    hc = h[:, :, 512 * c:512 * c + 512]
                    ve.scalar_tensor_tensor(hc, hc, ALPHA, o[:, :, :], ALU.mult, ALU.add).then_inc(free, 1)
                    ve.wait_ge(*emptied((name, c)))
                    half_stats(h, c)

            def rope(x1, x2, d1, d2, cos, sin, t1, t2, done):
                ve.tensor_tensor(t1, x1, cos, ALU.mult)
                link(ve.tensor_tensor(t2, x1, sin, ALU.mult))
                ve.tensor_tensor(d1, x2, sin, ALU.mult)
                link(ve.tensor_tensor(d2, x2, cos, ALU.mult))
                ve.tensor_tensor(d1, t1, d1, ALU.subtract)
                return ve.tensor_tensor(d2, d2, t2, ALU.add).then_inc(sems(done), 1)

            def heads(name, n, store, scale=1.0, mask=None, weight=None, behind=lambda i: None):
                for i in range(n + 2):
                    if i < n:
                        ve.wait_ge(*filled((name, "score", i)))
                        o, free = bank((name, "score", i))
                        s = o[:, :].rearrange("p (t k) -> p t k", t=NT)
                        if mask is not None:
                            if i >= 2:
                                ve.wait_ge(*filled((name, "probT", i - 2)))
                            ve.scalar_tensor_tensor(prob[:, i % 2, :, :], s, scale, mask(i), ALU.mult, ALU.add)\
                              .then_inc(free, 1)
                            ve.wait_ge(*emptied((name, "score", i)))
                            ve.tensor_reduce(smax[:, i % 2, :], prob[:, i % 2, :, :], AX.X, ALU.max, negate=True)\
                              .then_inc(sems("max_ready"), 1)
                        else:
                            link(ve.tensor_reduce(smax[:, i % 2, :], s, AX.X, ALU.max, negate=True))
                            ve.tensor_scalar(smax[:, i % 2, :], smax[:, i % 2, :], scale, None, ALU.mult)\
                              .then_inc(sems("max_ready"), 1)
                    if 1 <= i <= n:
                        m = i - 1
                        if mask is None:
                            ve.wait_ge(*emptied((name, "score", m)))
                        else:
                            ve.wait_ge(*L.next("exp_done"))
                        if weight is None:
                            link(ve.reciprocal(rsum[:, m % 2, :], ssum[:, m % 2, :]))
                            ve.tensor_tensor(prob[:, m % 2, :, :], prob[:, m % 2, :, :],
                                             bc(rsum[:, m % 2, :], 2, [P, NT, T]), ALU.mult)\
                              .then_inc(sems("prob_ready"), 1)
                            L.passed("prob_ready")
                        else:
                            ve.tensor_tensor(prob[:, m % 2, :, :], prob[:, m % 2, :, :], weight, ALU.mult)\
                              .then_inc(sems("prob_ready"), 1)
                            ve.wait_ge(*L.next("prob_ready"))
                            link(ve.tensor_reduce(ssum[:, m % 2, :], prob[:, m % 2, :, :], AX.X, ALU.add))
                            link(ve.reciprocal(rsum[:, m % 2, :], ssum[:, m % 2, :]))
                    if i >= 2:
                        store((name, "value", i - 2), i - 2)
                    behind(i)

            def store_T(first):
                def store(name, m):
                    copy(name, yT[HD * (m % 2):HD * (m % 2) + HD, first + m // 2, :], lambda o: o[0:HD, 0:T])
                return store

            def mixer(l):
                copies(("hT", "mix", l), hT, KD)
                at = 0
                for c in range(4):
                    w = Z_WIDTHS[c]
                    copy((("z", l), c), big[:, :, at:at + w], lambda o: o[:, :, 0:w])
                    at += w
                head_copies(("aT", l), 0, HD, 8)
                for c in range(2, 4):
                    ve.wait_ge(*emptied((("z", l), c)))
                ve.wait_ge(*L.next("head_gain_landed", 16))
                sq = att[:, 2560:2560 + NT * 640].rearrange("p (t n w) -> p t n w", t=NT, w=HD)
                zb = big[:, :, B_Q:B_Q + 640].rearrange("p t (n w) -> p t n w", w=HD)
                gb = head_gain[:, 0:640].rearrange("p (n w) -> p n w", w=HD)
                link(ve.tensor_tensor(sq, zb, zb, ALU.mult))
                link(ve.tensor_reduce(rstd[:, :, 0:10], sq, AX.X, ALU.add))
                inverse_root(rstd[:, :, 0:10], RMS_EPS, 1.0 / HD)
                for t in range(NT):
                    ins = ve.tensor_tensor(zb[:, t, :, :], zb[:, t, :, :], bc(rstd[:, t, 0:10], 2, [P, 10, HD]), ALU.mult)
                link(ins)
                for t in range(NT):
                    ins = ve.tensor_tensor(zb[:, t, :, :], zb[:, t, :, :], gb, ALU.mult)
                link(ins)
                tr = [att[:, 2560 + 320 * i:2560 + 320 * (i + 1)].rearrange("p (n w) -> p n w", w=32) for i in range(4)]
                cb, sn = table(C_COSB, 32), table(C_SINB, 32)
                for t in range(NT):
                    rope(zb[:, t, :, 0:32], zb[:, t, :, 32:64], zb[:, t, :, 0:32], zb[:, t, :, 32:64],
                         bc(cb[:, t, :], 1, [P, 10, 32]), bc(sn[:, t, :], 1, [P, 10, 32]), tr[2 * t], tr[2 * t + 1],
                         "b_rotated")
                ve.wait_ge(*L.next("b_rotated", 2))
                zc = big[:, :, C_DQ:C_DQ + DQ + DKV]
                sqc = att[:, 2560:2560 + NT * 384].rearrange("p (t n) -> p t n", t=NT)
                link(ve.tensor_tensor(sqc, zc, zc, ALU.mult))
                ve.tensor_reduce(rstd[:, :, 10], sqc[:, :, 0:DQ], AX.X, ALU.add)
                link(ve.tensor_reduce(rstd[:, :, 11], sqc[:, :, DQ:DQ + DKV], AX.X, ALU.add))
                link(ve.tensor_scalar(rstd[:, :, 11], rstd[:, :, 11], DQ / DKV, None, ALU.mult))
                inverse_root(rstd[:, :, 10:12], RMS_EPS, 1.0 / DQ)
                for t in range(NT):
                    for c, (a, w) in enumerate(((0, DQ), (DQ, DKV))):
                        ins = ve.scalar_tensor_tensor(zc[:, t, a:a + w], zc[:, t, a:a + w], rstd[:, t, 10 + c:11 + c],
                                                      head_gain[:, 640 + a:640 + a + w], ALU.mult, ALU.mult)
                ins.then_inc(sems("c_normed"), 1)
                ve.wait_ge(*L.next("c_normed"))
                cc, sc = table(C_COSC, 16), table(C_SINC, 16)
                tk = [att[:, 2560 + 32 * i:2592 + 32 * i].rearrange("p (t w) -> p t w", t=NT) for i in range(2)]
                kr = big[:, :, C_KR:C_KR + ROPE_C]
                rope(kr[:, :, 0:16], kr[:, :, 16:32], k_rope[:, :, 0:16], k_rope[:, :, 16:32], cc, sc, tk[0], tk[1],
                     "k_rotated")

                def head_bias(i):
                    ve.wait_ge(*L.next(f"bias{i % 2}_landed", 16))
                    return bias[:, i % 2, :, :]
                heads(("a", l), NA_HEADS, store_T(0), HD ** -0.5, mask=head_bias)
                head_copies(("bT", l), 0, HD, 10)
                heads(("b", l), GQA_HEADS, store_T(2), HD ** -0.5)
                copies(("cT", l), hT, 3)
                copy((("uq", l), 0), big[:, :, 0:384], lambda o: o[:, :, 0:384])
                copy((("ukv", l), 0), big[:, :, B_Q:B_Q + 512])
                ve.wait_ge(*emptied((("uq", l), 0)))
                qc = big[:, :, 0:384].rearrange("p t (n w) -> p t n w", w=96)
                tq = [att[:, 2560 + 64 * i:2624 + 64 * i].rearrange("p (n w) -> p n w", w=16) for i in range(4)]
                for t in range(NT):
                    rope(qc[:, t, :, 64:80], qc[:, t, :, 80:96], qc[:, t, :, 64:80], qc[:, t, :, 80:96],
                         bc(cc[:, t, :], 1, [P, 4, 16]), bc(sc[:, t, :], 1, [P, 4, 16]), tq[2 * t], tq[2 * t + 1],
                         "c_rotated")
                head_copies(("cqT", l), 0, 96, 4)
                head_copies(("ckT", l), 4, NOPE, 4)
                copy((("krT", l), 0), hv[64:96, 4:8, :], lambda o: bc(o[0:32, 0:T], 1, [32, 4, T]))
                heads(("c", l), MLA_HEADS, store_T(6), (NOPE + ROPE_C) ** -0.5)
                for b, branch in enumerate(("pa", "pb", "pc")):
                    for c in range(2):
                        g = big[:, :, ZQ + b * D + 512 * c:ZQ + b * D + 512 * c + 512]
                        ve.wait_ge(*L.at("gates_open", l + 1))
                        ve.wait_ge(*filled(((branch, l), c)))
                        o, free = bank(((branch, l), c))
                        m = mergedA[:, :, 512 * c:512 * c + 512]
                        if b == 0:
                            ve.tensor_tensor(m, g, o[:, :, :], ALU.mult).then_inc(free, 1)
                        else:
                            ve.tensor_tensor(g, g, o[:, :, :], ALU.mult).then_inc(free, 1)
                            ve.wait_ge(*emptied(((branch, l), c)))
                            ins = ve.tensor_tensor(m, m, g, ALU.add)
                            if (b, c) == (2, 1):
                                ins.then_inc(sems("merged"), 1)
                            else:
                                link(ins)
                copies(("mT", l), hT, KD)
                residual(("o", l))
                layer_norm()

            def cross(l):
                memory = big_flat[:, 0:2048].rearrange("p (t n) -> p t n", t=NT)
                memT = big_flat[:, 2048:4096].rearrange("p (k t) -> p k t", t=T)
                q = big_flat[:, 4096:6144].rearrange("p (t n) -> p t n", t=NT)
                k = big_flat[:, 6144:8192].rearrange("p (t n) -> p t n", t=NT)
                for c in range(3):
                    dst = k if c < 2 else memory
                    copy((("kv", l), c), dst[:, :, 512 * (c % 2):512 * (c % 2) + 512])
                copies(("hT", "mem", l), hT, KD)
                copies(("xkT", l), hv[:, 8:16, :], KD)
                for c in range(2):
                    copy((("q", l), c), q[:, :, 512 * c:512 * c + 512])
                copies(("xqT", l), hv[:, 0:8, :], KD)

                def store(name, m):
                    copy(name, yT[:, 2 * m:2 * m + 2, :], lambda o: o[:, :].rearrange("p (k t) -> p k t", t=T))
                heads(("x", l), MEM_HEADS, store, MEM_HD ** -0.5)
                residual(("xo", l))
                layer_norm()

            def route():
                ve.wait_ge(*filled(("router", 1)))
                o, free = bank(("router", 1))
                ve.tensor_copy(logit[:, :, :], o[:, 0:NT * 8].rearrange("p (t n) -> p t n", t=NT)).then_inc(free, 1)
                ve.wait_ge(*emptied(("router", 1)))
                for t in range(NT):
                    ins = ve.max(top[:, t, :], logit[:, t, :])
                link(ins)
                for t in range(NT):
                    ins = ve.max_index(top_i[:, t, :], top[:, t, :], logit[:, t, :])
                link(ins)
                ve.tensor_copy(top_f[:, :, :], top_i[:, :, :])
                ve.tensor_tensor(rstd[:, :, 0], top[:, :, 1], top[:, :, 0], ALU.subtract)\
                  .then_inc(sems("top_gap"), 1)
                ve.wait_ge(*L.next("second_exp"))
                link(ve.tensor_scalar(rstd[:, :, 2], rstd[:, :, 1], 1.0, None, ALU.add))
                link(ve.reciprocal(rstd[:, :, 3], rstd[:, :, 2]))
                link(ve.tensor_tensor(rstd[:, :, 4], rstd[:, :, 1], rstd[:, :, 3], ALU.mult))
                iota8 = const[:, C_IOTA8:C_IOTA8 + 8]
                for t in range(NT):
                    ve.tensor_scalar(tmp8[:, t, :], iota8, top_f[:, t, 0:1], rstd[:, t, 3:4], ALU.is_equal, ALU.mult)
                    ins = ve.tensor_scalar(gate[:, t, 0:8], iota8, top_f[:, t, 1:2], rstd[:, t, 4:5],
                                           ALU.is_equal, ALU.mult)
                link(ins)
                link(ve.tensor_tensor(gate[:, :, 0:8], gate[:, :, 0:8], tmp8[:, :, :], ALU.add))
                for t in range(NT):
                    ve.tensor_scalar(tmp8[:, t, :], iota8, top_f[:, t, 0:1], None, ALU.is_equal)
                    ins = ve.tensor_scalar(chosen[:, t, :], iota8, top_f[:, t, 1:2], None, ALU.is_equal)
                link(ins)
                ve.tensor_tensor(chosen[:, :, :], chosen[:, :, :], tmp8[:, :, :], ALU.add)\
                  .then_inc(sems("chosen_ready"), 1)
                ve.memset(place[:, :, :], -1.0)
                link(ve.memset(gate[:, :, 8:9], 0.0))
                ve.wait_ge(*L.next("chosen_ready"))
                ve.wait_ge(*filled(("places",)))
                o, free = bank(("places",))
                ve.tensor_tensor(place[:, :, 0:8], o[:, 0:16].rearrange("p (t n) -> p t n", t=NT), chosen[:, :, :],
                                 ALU.mult)
                ve.tensor_reduce(most[:, :], o[:, 16:24], AX.X, ALU.max).then_inc(free, 1)
                ve.wait_ge(*emptied(("places",)))
                link(ve.tensor_scalar(place[:, :, 0:8], place[:, :, 0:8], 1.0, None, ALU.subtract))
                ve.tensor_copy(most_i[:, :], most[:, :]).then_inc(sems("count_ready"), 1)
                ve.wait_ge(*L.next("count_ready"))

            def picks(col):
                slots = const[:, C_TIME:C_TIME + P]
                for t in range(NT):
                    ve.tensor_scalar(pick[:, t, :], slots, place[:, t, col], None, ALU.is_equal)
                    ins = ve.tensor_scalar(pick_gated[:, t, :], slots, place[:, t, col], gate[:, t, col],
                                           ALU.is_equal, ALU.mult)
                ins.then_inc(sems("picks_ready"), 1)
                L.passed("picks_ready")

            def few_copies(name):
                for g in range(2):
                    copy((name, g), few_T[:, 4 * g:4 * g + 4, :], lambda o: o[:, :].rearrange("p (k t) -> p k t", t=P))

            def few_body(ex):
                copy(("few", "put"), put_T, lambda o: o[:, 0:T])
                picks(bass.ds(ex + 1, 1))
                for c in range(HID_CHUNKS + 1):
                    if c < HID_CHUNKS:
                        ve.wait_ge(*L.next("silu_done"))
                        ve.wait_ge(*filled(("few", "up", c)))
                        o, free = bank(("few", "up", c))
                        ve.tensor_tensor(hid[:, c % 2, 0, :], silu[:, c % 2, 0, :], o[:, 0, 256:512], ALU.mult)\
                          .then_inc(free, 1)
                    if c:
                        copy(("few", "hidT", c - 1), hidT_few[:, 2 * c - 2:2 * c, :],
                             lambda o: o[:, 0:T].rearrange("p (k t) -> p k t", t=P))
                for i in range(2):
                    copy(("few", "down", i), few_y[:, 512 * i:512 * i + 512], lambda o: o[:, 0, :])
                few_copies("few_gather_next")
                for i in range(2):
                    ve.wait_ge(*filled(("few", "sum", i)))
                    o, free = bank(("few", "sum", i))
                    hc = h[:, :, 512 * i:512 * i + 512]
                    ve.tensor_tensor(hc, hc, o[:, :, :], ALU.add).then_inc(free, 1)

            def moe():
                ve.tensor_copy(h_rows, h[:, :, :]).then_inc(sems("rows_ready"), 1)
                ve.wait_ge(*L.next("rows_ready"))
                link(ve.tensor_scalar(h[:, :, :], h[:, :, :], ALPHA, None, ALU.mult))
                route()
                largest = ve.value_load(most_i[0:1, 0:1], min_val=0, max_val=T)
                start = dict(L.seen)
                with ve.If(largest < P + 1):
                    picks(slice(0, 1))
                    few_copies("few_gather")
                    with L.loop(N_EXPERTS, PER_FEW) as ex:
                        few_body(ex)
                    for i in range(2):
                        ring, b, _, use = jobs[("few", "sum", i)]
                        ve.wait_ge(*L.at(ring.emptied(b), use + (N_EXPERTS - 1) * PER_FEW[ring.emptied(b)]))
                few = dict(L.seen)
                L.seen = start
                with ve.Else():
                    with L.loop(N_EXPERTS, PER_EXPERT) as ex:
                        ffn_body(("ffn", 1), bass.ds(ex, 1))
                    for i in range(2):
                        ring, b, _, use = jobs[("ffn", 1), "down", i]
                        ve.wait_ge(*L.at(ring.emptied(b), use + (N_EXPERTS - 1) * PER_EXPERT[ring.emptied(b)]))
                    for name in surplus:
                        if name != "banks_filled" and surplus[name]:
                            ve.sem_inc(sems(name), surplus[name])
                    for name in few:
                        if few[name] - L.seen.get(name, 0):
                            ve.sem_inc(sems(name), few[name] - L.seen.get(name, 0))
                L.seen = few

            def ffn_body(name, col):
                for c in range(HID_CHUNKS + 1):
                    if c < HID_CHUNKS:
                        ve.wait_ge(*L.next("silu_done"))
                        ve.wait_ge(*filled((name, "up", c)))
                        o, free = bank((name, "up", c))
                        ve.tensor_tensor(hid[:, c % 2, :, :], silu[:, c % 2, :, :], o[:, :, 256:512], ALU.mult)\
                          .then_inc(free, 1)
                    if c:
                        copy((name, "hidT", c - 1), hidT[:, 2 * c - 2:2 * c, :],
                             lambda o: o[:, :].rearrange("p (k t) -> p k t", t=T))
                for i in range(2):
                    ve.wait_ge(*filled((name, "down", i)))
                    o, free = bank((name, "down", i))
                    for t in range(NT):
                        hc = h[:, t, 512 * i:512 * i + 512]
                        ins = ve.scalar_tensor_tensor(hc, o[:, t, :], gate[:, t, col], hc, ALU.mult, ALU.add)
                    ins.then_inc(free, 1)

            def ffn(l):
                copies(("hT", "ffn", l), hT, KD)
                if l == 0:
                    ve.memset(gate[:, :, 8:9], 1.0)
                    link(ve.tensor_scalar(h[:, :, :], h[:, :, :], ALPHA, None, ALU.mult))
                    ffn_body(("ffn", 0), slice(8, 9))
                    for i in range(2):
                        ve.wait_ge(*emptied((("ffn", 0), "down", i)))
                else:
                    moe()
                for c in range(2):
                    half_stats(h, c)
                layer_norm()

            def even():
                pre_norm()
                copies(("eT",), hT, KD)
                ssm_params()
                for c in range(6):
                    copy((("ez",), c), wide[:, :, 512 * c:512 * c + 512])
                ve.wait_ge(*emptied((("ez",), 3)))
                qk = wide[:, :, 0:2048].rearrange("p t (n w) -> p t n w", w=HD)
                t1, t2 = [att[:, 5120 + 256 * i:5376 + 256 * i].rearrange("p (n w) -> p n w", w=8) for i in range(2)]
                t3, t4 = [att[:, 5632 + 256 * i:5888 + 256 * i].rearrange("p (n w) -> p n w", w=8) for i in range(2)]
                c2, s2 = table(C_COS2, 8), table(C_SIN2, 8)
                for t, (ta, tb) in enumerate(((t1, t2), (t3, t4))):
                    rope(qk[:, t, :, 0:8], qk[:, t, :, 8:16], qk[:, t, :, 0:8], qk[:, t, :, 8:16],
                         bc(c2[:, t, :], 1, [P, 32, 8]), bc(s2[:, t, :], 1, [P, 32, 8]), ta, tb, "e_rotated")
                dmask = table(C_DMASK, T)
                dmul = table(C_DMUL, T)

                def store(name, m):
                    ve.wait_ge(*filled(name))
                    o, free = bank(name)
                    for t in range(NT):
                        ins = ve.tensor_scalar(e(t, E_Q + m * HD, HD), o[:, t * HD:(t + 1) * HD],
                                               rsum[:, m % 2, t:t + 1], None, ALU.mult)
                    ins.then_inc(free, 1)

                def tiles_out(g, j):
                    copy((("ehT", g, j), 0), head_tiles(g)[j // 4][0:HD, j % 4:j % 4 + 2, :],
                         lambda o: o[0:HD, :].rearrange("p (k t) -> p k t", t=T))

                def behind(i):
                    for g, j in groups_next(i):
                        tiles_out(g, j)
                for j in range(0, 8, 2):
                    tiles_out(0, j)
                heads("e", ATT_HEADS, store, HD ** -0.5, mask=lambda i: dmask, weight=dmul, behind=behind)
                ve.wait_ge(*L.next("gates_silu"))
                ve.wait_ge(*emptied(("e", "value", ATT_HEADS - 1)))
                q_out = wide[:, :, E_Q:E_Q + D]
                g_att = wide[:, :, E_G:E_G + D]
                ve.tensor_tensor(g_att, g_att, q_out, ALU.mult).then_inc(sems("ssm_space"), 1)
                ve.wait_ge(*L.next("ssm_space"))
                copies(("uT",), hT, 4)
                ssm()
                copies(("gT",), hT, 4)
                ve.wait_ge(*filled((("glu",), 0)))
                o, free = bank((("glu",), 0))
                z = rot_in_flat
                ve.tensor_tensor(z, o[:, :, :], bc(ssm_vec[:, 1, :], 1, [P, NT, SSM_W]), ALU.add).then_inc(free, 1)
                ve.wait_ge(*L.next("glu_sigmoid"))
                u = wide[:, :, E_U:E_U + SSM_W]
                link(ve.tensor_tensor(u, u, z, ALU.mult))
                ve.wait_ge(*L.next("ssm_gate_silu"))
                ve.tensor_tensor(u, u, wide[:, :, E_GS:E_GS + SSM_W], ALU.mult).then_inc(sems("even_merged"), 1)
                copies(("smT",), even_merged_parts[2], 4)
                copy((("eo",), 0), y_out[:, :, 0:512])
                ve.wait_ge(*emptied((("eo",), 0)))
                half_stats(y_out, 0)
                for t in range(NT):
                    copy((("eo", 1), t), y_out[:, t, 512:1024], lambda o: o[:, :])
                    ve.wait_ge(*emptied((("eo", 1), t)))
                half_stats(y_out, 1)
                post_norm()

            rot_in_flat = big_flat[:, 2048:3072].rearrange("p (t n) -> p t n", t=NT)

            def tt(o, a, b, op):
                link(ve.tensor_tensor(o, a, b, op))

            def ts(o, a, s1, op1, s2=None, op2=ALU.bypass):
                link(ve.tensor_scalar(o, a, s1, s2, op1, op2))

            def ssm_params():
                ve.wait_ge(*L.next("ssm_par_landed", 16))
                a_re, a_im = ssm_par[:, 0, :], ssm_par[:, 1, :]
                dt, re, im, rho, tau, k, sn, cs, lr, li, den, cr, ci, x, y2, th = ssm_v

                ve.wait_ge(*L.next("ssm_dt"))
                tt(im, a_im, dt, ALU.mult)
                ve.tensor_tensor(re, a_re, dt, ALU.mult).then_inc(sems("ssm_re"), 1)
                ts(k, im, 1 / TWO_PI, ALU.mult)
                ts(k, k, ROUND, ALU.add, ROUND, ALU.subtract)
                link(ve.scalar_tensor_tensor(th, k, -TWO_PI_HI, im, ALU.mult, ALU.add))
                link(ve.scalar_tensor_tensor(th, k, -TWO_PI_LO, th, ALU.mult, ALU.add))
                ts(tau, th, 1 / TWO_PI, ALU.mult)
                ts(x, tau, 0.25, ALU.add)
                ts(k, x, ROUND, ALU.add, ROUND, ALU.subtract)
                ve.tensor_tensor(x, x, k, ALU.subtract).then_inc(sems("ssm_phase"), 1)
                ve.wait_ge(*L.next("ssm_phase"))
                tt(den, a_re, a_re, ALU.mult)
                tt(y2, a_im, a_im, ALU.mult)
                tt(den, den, y2, ALU.add)
                link(ve.reciprocal(den, den))
                ve.wait_ge(*L.next("ssm_lam"))
                tt(lr, rho, cs, ALU.mult)
                tt(li, rho, sn, ALU.mult)
                ts(lr, lr, 1.0, ALU.subtract)
                tt(cr, lr, a_re, ALU.mult)
                tt(y2, li, a_im, ALU.mult)
                tt(cr, cr, y2, ALU.add)
                tt(cr, cr, den, ALU.mult)
                tt(ci, li, a_re, ALU.mult)
                tt(y2, lr, a_im, ALU.mult)
                tt(ci, ci, y2, ALU.subtract)
                tt(ci, ci, den, ALU.mult)

            def ssm():
                rho, cr, ci = ssm_v[3], ssm_v[11], ssm_v[12]
                ve.wait_ge(*L.next("ssm_w_landed", 16))
                ta = tmp_flat(0)
                tb = tmp_flat(1)
                tc = tmp_flat(2)
                cre, cim = ssm_c[:, 0, :, :], ssm_c[:, 1, :, :]
                crb, cib = bc(cr, 2, [P, SSM_TILES, 32]), bc(ci, 2, [P, SSM_TILES, 32])
                tt(ta, cre, cib, ALU.mult)
                tt(tb, cim, crb, ALU.mult)
                tt(ta, ta, tb, ALU.add)
                tt(tb, cre, crb, ALU.mult)
                tt(tc, cim, cib, ALU.mult)
                tt(cre, tb, tc, ALU.subtract)
                ts(cim, ta, -1.0, ALU.mult)
                ve.wait_ge(*L.next("ssm_vec_landed", 16))
                du = mergedA[:, :, 0:SSM_W]
                ve.wait_ge(*emptied((("er",), 2)))
                ve.tensor_tensor(du, wide[:, :, E_U:E_U + SSM_W], bc(ssm_vec[:, 0, :], 1, [P, NT, SSM_W]), ALU.mult)

                def angles(b):
                    ve.wait_ge(*L.next("turns_ready"))
                    S = sinT[:, b % 2, :, :]
                    ve.scalar_tensor_tensor(S, S, ROUND, cosT[:, b % 2, :, :], ALU.subtract, ALU.subtract)\
                      .then_inc(sems("angles_ready"), 1)

                angles(0)
                for b in range(SSM_TILES // 2):
                    ve.wait_ge(*L.next("sincos_ready"))
                    S, C = sinT[:, b % 2, :, :], cosT[:, b % 2, :, :]
                    ve.wait_ge(*filled(("Bu", b, 0)))
                    o_re, free_re = bank(("Bu", b, 0))
                    ve.wait_ge(*filled(("Bu", b, 1)))
                    o_im, free_im = bank(("Bu", b, 1))
                    bre = o_re[:, :].rearrange("p (i t) -> p i t", i=2)
                    bim = o_im[:, :].rearrange("p (i t) -> p i t", i=2)
                    wr, wi = rot_in[:, 0, :, :], rot_in[:, 1, :, :]
                    tt(wr, C, bre, ALU.mult)
                    tt(tmpA, S, bim, ALU.mult)
                    ve.tensor_tensor(wi, C, bim, ALU.mult).then_inc(free_im, 1)
                    ve.tensor_tensor(tmpB, S, bre, ALU.mult).then_inc(free_re, 1)
                    ve.wait_ge(*emptied(("Bu", b, 0)))
                    ve.wait_ge(*emptied(("Bu", b, 1)))
                    tt(wr, wr, tmpA, ALU.add)
                    tt(wi, wi, tmpB, ALU.subtract)
                    if b:
                        ve.wait_ge(*L.next("im_ready"))
                    for c, w in enumerate((wr, wi)):
                        for i in range(2):
                            j = 2 * b + i
                            ins = ve.tensor_tensor_scan(scanned[:, c, i, :], rho[:, j:j + 1].to_broadcast([P, T]),
                                                        w[:, i, :], 0.0, ALU.mult, ALU.add)
                    ins.then_inc(sems("scans_ready"), 1)
                    if b + 1 < SSM_TILES // 2:
                        angles(b + 1)
                    ve.wait_ge(*L.next("scans_ready"))
                    rr, ri = scanned[:, 0, :, :], scanned[:, 1, :, :]
                    if b:
                        ve.wait_ge(*L.next("states_used"))
                    sr = ssm_state[:, 0, :, :]
                    tt(sr, C, rr, ALU.mult)
                    tt(tmpA, S, ri, ALU.mult)
                    ve.tensor_tensor(sr, sr, tmpA, ALU.subtract).then_inc(sems("re_ready"), 1)
                    ve.wait_ge(*L.next("re_ready"))
                ve.wait_ge(*filled(("ssm_y",)))
                o, free = bank(("ssm_y",))
                ve.tensor_tensor(wide[:, :, E_U:E_U + SSM_W], o[:, :, :], du, ALU.add).then_inc(free, 1)

            def tmp_flat(i):
                return big_flat[:, at1 + 512 * i:at1 + 512 * (i + 1)].rearrange("p (j n) -> p j n", n=32)

            def odd():
                pre_norm()
                copies(("dT",), hT, KD)
                u = big_flat[:, 0:4096].rearrange("p (t n) -> p t n", t=NT)
                g = big_flat[:, 4096:8192].rearrange("p (t n) -> p t n", t=NT)
                for c in range(4):
                    copy((("dz",), c), u[:, :, 512 * c:512 * c + 512])
                copies("mixT", att[:, 0:4096].rearrange("p (k t) -> p k t", t=T), 16)
                ve.wait_ge(*L.next("pool_scale_landed", 16))
                for gi in range(4):
                    ta = att[:, 4096 + 1024 * (gi % 2):5120 + 1024 * (gi % 2)].rearrange("p (t n) -> p t n", t=NT)
                    ve.wait_ge(*filled((("pw", gi), 0)))
                    o, free = bank((("pw", gi), 0))
                    ve.tensor_tensor(ta, o[:, :, :], bc(pool_scale[:, 512 * gi:512 * gi + 512], 1, [P, NT, 512]),
                                     ALU.mult).then_inc(free, 1)
                    ve.wait_ge(*emptied((("pw", gi), 0)))
                    ve.wait_ge(*emptied((("dz",), 4 + gi)))
                    gg = g[:, :, 512 * gi:512 * gi + 512]
                    ins = ve.tensor_tensor(gg, gg, ta, ALU.mult)
                ins.then_inc(sems("odd_gated"), 1)
                copies(("odT",), att[:, 0:4096].rearrange("p (k t) -> p k t", t=T), 16)
                for c in range(2):
                    copy((("do",), c), y_out[:, :, 512 * c:512 * c + 512])
                    ve.wait_ge(*emptied((("do",), c)))
                    half_stats(y_out, c)
                post_norm()

            ve.wait_ge(*L.next("x_landed", 16))
            for c in range(2):
                half_stats(h, c)
            layer_norm()
            ve.wait_ge(*L.next("const_landed", 16))
            for l in range(DEPTH):
                if on(f"mix{l}"):
                    mixer(l)
                if on(f"mem{l}"):
                    cross(l)
                if on(f"ffn{l}"):
                    ffn(l)
            if on("even"):
                even()
            if on("odd"):
                odd()

        @block.scalar
        def _(act):
            L = Line(act, sems)
            filled, bank, emptied = consumer(L)

            def transposed(name, m):
                act.wait_ge(*filled((name, "probT", m)))
                o, free = bank((name, "probT", m))
                act.activation(probT[:, m % 2, :, :], o[:, :].rearrange("p (j t) -> p j t", j=NT), ACT.Copy)\
                   .then_inc(free, 1)

            def beside(product):
                name, c = product
                if name[0] == "g":
                    return big[:, :, ZQ + 512 * c:ZQ + 512 * c + 512]
                if name[0] == "v":
                    return big_flat[:, 0:2048].rearrange("p (t n) -> p t n", t=NT)[:, :, 512:1024]
                return wide[:, :, E_G + 512 * c:E_G + 512 * c + 512]

            def streamed(where):
                for product in ended_in.get(where, ()):
                    act.wait_ge(*filled(product))
                    o, free = bank(product)
                    act.activation(beside(product), o[:, :, :], ACT.Copy).then_inc(free, 1)

            def exps(name, n, scale, masked):
                for i in range(n + 1):
                    if i == n:
                        transposed(name, i - 1)
                        break
                    act.wait_ge(*L.next("max_ready"))
                    ring, b, _, _ = jobs[(name, "score", i)]
                    for t in range(NT):
                        p = prob[:, i % 2, t, :]
                        src = p if masked else ring.views[b][:, t * T:(t + 1) * T]
                        ins = act.activation(p, src, ACT.Exp, bias=smax[:, i % 2, t:t + 1],
                                             scale=1.0 if masked else scale, accum_out=ssum[:, i % 2, t:t + 1])
                    ins.then_inc(sems("exp_done") if masked else sems(ring.emptied(b)), 1)
                    if i:
                        transposed(name, i - 1)
                    streamed((name, i))

            def copies(name, dst, k_tiles):
                for j in k_tiles:
                    act.wait_ge(*filled((name, j)))
                    o, free = bank((name, j))
                    at = j - k_tiles[0]
                    act.activation(dst[:, at:at + 2, :], o[:, :].rearrange("p (k t) -> p k t", t=T), ACT.Copy)\
                       .then_inc(free, 1)

            def root(a=0, b=1):
                act.wait_ge(*L.next("variance_ready"))
                act.activation(rstd[:, :, a:b], rstd[:, :, a:b], ACT.Sqrt).then_inc(sems("root_ready"), 1)

            def gates(name, chunks, func, dst):
                for c in chunks:
                    act.wait_ge(*filled((name, c)))
                    o, free = bank((name, c))
                    act.activation(dst(c), o[:, :, :], func).then_inc(free, 1)

            def ffn_body(name):
                for c in range(HID_CHUNKS):
                    act.wait_ge(*filled((name, "up", c)))
                    o, _ = bank((name, "up", c))
                    act.activation(silu[:, c % 2, :, :], o[:, :, 0:256], ACT.Silu).then_inc(sems("silu_done"), 1)

            root()
            for l in range(DEPTH):
                if on(f"mix{l}"):
                    root(0, 10)
                    root(10, 12)
                    streamed(("ahead", l))
                    exps(("a", l), NA_HEADS, 1.0, True)
                    exps(("b", l), GQA_HEADS, HD ** -0.5, False)
                    for c in range(6):
                        act.wait_ge(*emptied((("g", l), c)))
                    act.activation(big[:, :, ZQ:ZQ + 3 * D], big[:, :, ZQ:ZQ + 3 * D], ACT.Sigmoid)\
                       .then_inc(sems("gates_open"), 1)
                    exps(("c", l), MLA_HEADS, (NOPE + ROPE_C) ** -0.5, False)
                    if on(f"mem{l}"):
                        copies(("memT", l), big_flat[:, 2048:4096].rearrange("p (k t) -> p k t", t=T), range(0, KD, 2))
                    root()
                if on(f"mem{l}"):
                    exps(("x", l), MEM_HEADS, MEM_HD ** -0.5, False)
                    root()
                if on(f"ffn{l}"):
                    if l == 0:
                        ffn_body(("ffn", l))
                    else:
                        act.wait_ge(*L.next("top_gap"))
                        act.activation(rstd[:, :, 1], rstd[:, :, 0], ACT.Exp).then_inc(sems("second_exp"), 1)
                        act.wait_ge(*L.next("count_ready"))
                        largest = act.value_load(most_i[0:1, 0:1], min_val=0, max_val=T)
                        with act.If(largest < P + 1):
                            with L.loop(N_EXPERTS, PER_FEW):
                                for c in range(HID_CHUNKS):
                                    act.wait_ge(*filled(("few", "up", c)))
                                    o, _ = bank(("few", "up", c))
                                    act.activation(silu[:, c % 2, 0, :], o[:, 0, 0:256], ACT.Silu)\
                                       .then_inc(sems("silu_done"), 1)
                        with act.Else():
                            with L.loop(N_EXPERTS, PER_EXPERT):
                                ffn_body(("ffn", l))
                    root()
            if on("even"):
                root()
                dt, re, im, rho, tau, k, sn, cs = [ssm_s[:, i, :] for i in range(8)]
                x, th = ssm_s[:, 13, :], ssm_s[:, 15, :]
                act.wait_ge(*L.next("ssm_par_landed", 16))
                act.activation(dt, ssm_par[:, 2, :], ACT.Exp).then_inc(sems("ssm_dt"), 1)
                act.wait_ge(*L.next("ssm_re"))
                act.activation(rho, re, ACT.Exp)
                act.wait_ge(*L.next("ssm_phase"))
                act.activation(sn, tau, ACT.Sin, scale=TURN)
                act.activation(cs, x, ACT.Sin, scale=TURN).then_inc(sems("ssm_lam"), 1)
                exps("e", ATT_HEADS, 1.0, True)
                for c in range(2):
                    act.wait_ge(*emptied((("er",), c)))
                act.activation(wide[:, :, E_G:E_G + D], wide[:, :, E_G:E_G + D], ACT.Silu)\
                   .then_inc(sems("gates_silu"), 1)
                streamed("behind even's heads")
                for c in range(2, 4):
                    act.wait_ge(*emptied((("er",), c)))
                act.activation(wide[:, :, E_GS:E_GS + SSM_W], wide[:, :, E_GS:E_GS + SSM_W], ACT.Silu)\
                   .then_inc(sems("ssm_gate_silu"), 1)
                act.wait_ge(*L.next("ssm_space"))
                act.wait_ge(*L.next("biases_set"))
                time = const[:, C_TIME:C_TIME + T]
                for b in range(SSM_TILES // 2):
                    S, C = sinT[:, b % 2, :, :], cosT[:, b % 2, :, :]
                    if b >= 2:
                        act.wait_ge(*L.next("re_ready"))
                        act.wait_ge(*L.next("im_ready"))
                    for i in range(2):
                        ins = act.activation(C[:, i, :], time, ACT.Identity, scale=tau[:, 2 * b + i:2 * b + i + 1])
                    ins.then_inc(sems("scalar_step"), 1)
                    act.wait_ge(*L.next("scalar_step"))
                    act.activation(S, C, ACT.Identity, bias=bias_values[:, 0:1]).then_inc(sems("turns_ready"), 1)
                    act.wait_ge(*L.next("angles_ready"))
                    act.activation(C, S, ACT.Abs).then_inc(sems("scalar_step"), 1)
                    act.wait_ge(*L.next("scalar_step"))
                    act.activation(S, S, ACT.Sin, scale=-TURN)
                    act.activation(C, C, ACT.Sin, scale=-TURN, bias=bias_values[:, 1:2])\
                       .then_inc(sems("sincos_ready"), 1)
                    if b < 2:
                        copies(("emT",), even_merged_parts[b], (4 * b, 4 * b + 2))
                act.wait_ge(*emptied(("ssm_y",)))
                u = wide[:, :, E_U:E_U + SSM_W]
                act.activation(u, u, ACT.Gelu_apprx_tanh).then_inc(sems("gelu_done"), 1)
                act.wait_ge(*emptied((("glu",), 0)))
                z = big_flat[:, 2048:3072].rearrange("p (t n) -> p t n", t=NT)
                act.activation(z, z, ACT.Sigmoid).then_inc(sems("glu_sigmoid"), 1)
                root()
            if on("odd"):
                root()
                g = big_flat[:, 4096:8192].rearrange("p (t n) -> p t n", t=NT)
                gates(("dz",), range(4, 8), ACT.Silu, lambda c: g[:, :, 512 * (c - 4):512 * (c - 3)])
                root()

        @block.gpsimd
        def _(gp):
            L = Line(gp, sems)
            filled, bank, emptied = consumer(L)
            norms = [1]
            gp.memset(bias_values[:, 0:1], ROUND)
            gp.memset(bias_values[:, 1:2], TURN / 4).then_inc(sems("biases_set"), 1)

            def norm_params():
                n = norms[0]
                norms[0] += 1
                if n >= 2:
                    gp.wait_ge(*L.at("normed", n - 1))
                gp.dma_start(norm_par[:, n % 2, :, :].rearrange("p a n -> p (a n)"),
                             d["norms"][n:n + 1, :].to_broadcast([P, 2 * D])).then_inc(sems(f"norm_par{n % 2}_landed"), 16)

            gp.wait_ge(*L.next("const_landed", 16))
            norm_params()
            gp.dma_start(router_w[:, :, :], d["router"].rearrange("p (k n) -> p k n", n=N_EXPERTS))\
              .then_inc(sems("router_landed"), 16)
            gp.dma_start(ssm_par[:, :, :], d["ssm_par"].rearrange("p (c j) -> p c j", c=3))\
              .then_inc(sems("ssm_par_landed"), 16)
            for l in range(DEPTH):
                if on(f"mix{l}"):
                    if l:
                        gp.wait_ge(*L.at("normed", 2))
                    gp.dma_start(head_gain[:, :], d["head_gain"][l:l + 1, :].to_broadcast([P, 1024]))\
                      .then_inc(sems("head_gain_landed"), 16)
                    for i in range(NA_HEADS):
                        if i >= 2:
                            gp.wait_ge(*emptied((("a", l), "score", i - 2)))
                        elif l:
                            gp.wait_ge(*emptied((("a", l - 1), "score", i + 2)))
                        gp.dma_start(bias[:, i % 2, :, :], d["bias"][l, i].rearrange("p (t k) -> p t k", t=NT))\
                          .then_inc(sems(f"bias{i % 2}_landed"), 16)
                    norm_params()
                if on(f"mem{l}"):
                    gp.wait_ge(*L.at("merged", l + 1))
                    gp.dma_start(big_flat[:, 0:2048].rearrange("p (t n) -> p t n", t=NT),
                                 d["mem"].rearrange("(t p) n -> p t n", p=P)).then_inc(sems("mem_landed"), 16)
                    norm_params()
                if on(f"ffn{l}"):
                    norm_params()
            if on("even"):
                gp.wait_ge(*L.at("normed", 7))
                gp.dma_start(att[:, 2048:4096], d["ssm_w"]).then_inc(sems("ssm_w_landed"), 16)
                gp.dma_start(att[:, 4096:5120], d["ssm_vec"][0:1, :].to_broadcast([P, 1024]))\
                  .then_inc(sems("ssm_vec_landed"), 16)
                norm_params()
                norm_params()
                ta, tb = pool_tmp
                gp.wait_ge(*L.next("ssm_space"))
                for b in range(SSM_TILES // 2):
                    S, C = sinT[:, b % 2, :, :], cosT[:, b % 2, :, :]
                    gp.wait_ge(*L.next("scans_ready"))
                    if b:
                        gp.wait_ge(*L.next("states_used"))
                    gp.tensor_tensor(ta, C, scanned[:, 1, :, :], ALU.mult)
                    gp.tensor_tensor(tb, S, scanned[:, 0, :, :], ALU.mult).then_inc(sems("pool_step"), 1)
                    gp.wait_ge(*L.next("pool_step"))
                    gp.tensor_tensor(ssm_state[:, 1, :, :], ta, tb, ALU.add).then_inc(sems("im_ready"), 1)
                    gp.wait_ge(*L.next("im_ready"))
            if on("odd"):
                gp.wait_ge(*L.at("normed", 9))
                gp.dma_start(att[:, 4096:6144], d["window"]).then_inc(sems("window_landed"), 16)
                gp.dma_start(pool_scale, d["pool_scale"][0:1, :].to_broadcast([P, POOL_W]))\
                  .then_inc(sems("pool_scale_landed"), 16)
                norm_params()

        @block.sync
        def _(sp):
            L = Line(sp, sems)
            n = [0]

            def load(src, width):
                i = n[0]
                n[0] += 1
                s = i % NSLOT
                if i >= NSLOT:
                    sp.wait_ge(*L.at(f"slot{s}_used", i // NSLOT))
                sp.dma_start(weights[:, s, 0:width], src).then_inc(sems(f"slot{s}_landed"), 16)

            def stream(src, k_tiles, widths, group):
                for c, k0, nk, w, off in weight_tiles(k_tiles, widths, group):
                    load(src[:, off:off + nk * w], nk * w)

            def expert(up, down):
                for c in range(HID_CHUNKS):
                    load(up[:, c * 4096:(c + 1) * 4096], 4096)
                k0 = 0
                for nk in DOWN_GROUPS:
                    load(down[:, k0 * 1024:(k0 + nk) * 1024], nk * 1024)
                    k0 += nk

            sp.dma_start(h[:, :, :], d["x"].rearrange("(t p) n -> p t n", p=P)).then_inc(sems("x_landed"), 16)
            sp.dma_start(norm_par[:, 0, :, :].rearrange("p a n -> p (a n)"), d["norms"][0:1, :].to_broadcast([P, 2 * D]))\
              .then_inc(sems("first_norm_landed"), 16)
            sp.dma_start(const[:, :], d["const"]).then_inc(sems("const_landed"), 16)
            sp.wait_ge(*L.next("first_norm_landed", 16))
            for l in range(DEPTH):
                if on(f"mix{l}"):
                    stream(d["w_in"][l], KD, Z_WIDTHS, KD)
                    stream(d["w_uq"][l], 2, [384], 2)
                    stream(d["w_ukv"][l], 1, [512], 1)
                    stream(d["w_pa"][l], 2, [512] * 2, 2)
                    stream(d["w_pb"][l], 4, [1024], 4)
                    stream(d["w_pc"][l], 2, [1024], 2)
                    stream(d["w_out"][l], KD, [512] * 2, KD)
                if on(f"mem{l}"):
                    kv = d["mem_wkv"][l]
                    stream(kv[:, 0:3 * KD * 512], KD, [512] * 3, KD)
                    stream(d["mem_wq"][l], KD, [512] * 2, KD)
                    stream(kv[:, 3 * KD * 512:], KD, [512], KD)
                    stream(d["mem_wo"][l], KD, [512] * 2, KD)
                if on(f"ffn{l}"):
                    if l == 0:
                        expert(d["ffn_up"][0], d["ffn_down"][0])
                    else:
                        before = n[0]
                        with L.loop(N_EXPERTS, PER_EXPERT) as ex:
                            expert(d["moe_up"][bass.ds(ex, 1)].rearrange("e p n -> p (e n)"),
                                   d["moe_down"][bass.ds(ex, 1)].rearrange("e p n -> p (e n)"))
                        n[0] += (N_EXPERTS - 1) * (n[0] - before)
            if on("even"):
                stream(d["even_in"], KD, [512] * 10, KD)
                stream(d["even_out_att"], KD, [512] * 2, KD)
                stream(d["glu"], 4, [512], 4)
                stream(d["even_out_ssm"], 4, [512] * 2, 4)
            if on("odd"):
                stream(d["odd_in"], KD, [512] * 8, KD)
                for gi in range(4):
                    stream(d["pool_w"][gi], 4, [512], 4)
                stream(d["odd_out"], 16, [512] * 2, 8)
            assert n[0] == tiles_used[0], (n[0], tiles_used[0])
            n_norms = {"emb": 1, "even": 9, "odd": 11}.get(STAGES[n_stages - 1], n_stages)
            sp.wait_ge(*L.at("normed", n_norms))
            sp.dma_start(out.rearrange("a (t p) n -> p (a t) n", p=P), h[:, :, :]).then_inc(sems("out_stored"), 16)
            sp.wait_ge(sems("out_stored"), 16)


def _packed(w, widths, group):
    k, n = w.shape
    v = w.reshape(k // P, P, n).transpose(1, 0, 2)
    out, at = np.empty((P, k // P * n), w.dtype), 0
    starts = [sum(widths[:c]) for c in range(len(widths))]
    for c, k0, nk, width, off in weight_tiles(k // P, widths, group):
        out[:, off:off + nk * width] = v[:, k0:k0 + nk, starts[c]:starts[c] + width].reshape(P, nk * width)
    return out


def _experts(up, down):
    e = up.shape[0]
    u = up.reshape(e, KD, P, 2, HID_CHUNKS, 256).transpose(0, 2, 4, 1, 3, 5).reshape(e, P, HID_CHUNKS * 4096)
    w = down.reshape(e, KF, P, D).transpose(0, 2, 1, 3).reshape(e, P, KF * D)
    return np.ascontiguousarray(u), np.ascontiguousarray(w)


def _window_index():
    rows = T // GRID_W
    r, c = np.arange(T) // GRID_W, np.arange(T) % GRID_W
    first = np.clip(c - NA_COLS // 2, 0, GRID_W - NA_COLS)
    inside = (c[None, :] >= first[:, None]) & (c[None, :] < first[:, None] + NA_COLS)
    dr = r[None, :] - r[:, None] + 7
    dc = np.clip(c[None, :] - c[:, None] + NA_COLS - 1, 0, 2 * NA_COLS - 2)
    assert rows <= 8
    return inside, dr, dc


def _tiles(a):
    return a.reshape(NT, P, -1).transpose(1, 0, 2).reshape(P, -1)


def _constants():
    c = np.zeros((P, C_END), np.float32)
    c[:, C_ID:C_ID + P] = np.eye(P)
    t = np.arange(T)
    row, col = (t // GRID_W).astype(np.float32), (t % GRID_W).astype(np.float32)

    def axial(rot):
        n = rot // 4
        inv = (np.float32(ROPE_THETA) ** (-np.arange(n, dtype=np.float32) / np.float32(n))).astype(np.float32)
        return np.concatenate([row[:, None] * inv, col[:, None] * inv], axis=-1)
    for at, rot in ((C_COSB, HD), (C_COSC, ROPE_C)):
        ang = axial(rot)
        w = NT * rot // 2
        c[:, at:at + w] = _tiles(np.cos(ang))
        c[:, at + w:at + 2 * w] = _tiles(np.sin(ang))
    inv = (np.float32(THETA_2) ** (-np.arange(0, ROT, 2, dtype=np.float32) / np.float32(ROT))).astype(np.float32)
    ang = t.astype(np.float32)[:, None] * inv
    c[:, C_COS2:C_COS2 + 16] = _tiles(np.cos(ang))
    c[:, C_SIN2:C_SIN2 + 16] = _tiles(np.sin(ang))
    delta = t[:, None] - t[None, :]
    count = sum(((delta >= 0) & (delta <= w) & (delta % dil == 0)).astype(np.float32)
                for w, dil in ((128, 1), (512, 4), (2048, 16)))
    c[:, C_DMASK:C_DMASK + NT * T] = _tiles(np.where(count > 0, 0.0, NEG).astype(np.float32))
    c[:, C_DMUL:C_DMUL + NT * T] = _tiles(count)
    c[:, C_TIME:C_TIME + T] = t
    c[:, C_IOTA8:C_IOTA8 + 8] = np.arange(8)
    c[:, C_UPPER:C_UPPER + P] = np.triu(np.ones((P, P)))
    c[:, C_ONES:C_ONES + P] = 1.0
    return c


def _windows():
    t = np.arange(T)
    out = np.zeros((P, 4, NT, T), np.float32)
    for g, w in enumerate(POOL_WINDOWS):
        d = t[None, :] - t[:, None]
        m = ((d >= 0) & (d < w)) / np.minimum(t[None, :] + 1, w) - (d == 0)
        out[:, g] = m.reshape(NT, P, T).transpose(1, 0, 2)
    return out.reshape(P, -1)


def _layout(i):
    a = {k: np.asarray(v) for k, v in i.items()}
    f = np.float32
    d = {"x": a["x"].reshape(T, D), "mem": a["mem"].reshape(T, D), "const": _constants(), "window": _windows()}
    zero = np.zeros(D, f)
    norms = [(a["emb_ln_g"], a["emb_ln_b"])]
    norms += [(a["ln_g"][l, j], a["ln_b"][l, j]) for l in range(DEPTH) for j in range(3)]
    for l in range(DEPTH):
        norms += [(a["pre_norm_2"][l], zero), (a["post_norm_2"][l], zero)]
    d["norms"] = np.stack([np.concatenate(p) for p in norms])
    gains = np.zeros((DEPTH, 1024), f)
    for l in range(DEPTH):
        gains[l] = np.concatenate([np.tile(a["gqa_q_norm"][l], GQA_HEADS), np.tile(a["gqa_k_norm"][l], GQA_KV),
                                   a["mla_q_norm"][l], a["mla_kv_norm"][l]])
    d["head_gain"] = gains
    inside, dr, dc = _window_index()
    b = np.where(inside, a["na_rpb"][:, :, dr, dc], f(NEG)).astype(f)
    d["bias"] = np.ascontiguousarray(
        b.reshape(DEPTH, NA_HEADS, NT, P, T).transpose(0, 1, 3, 2, 4).reshape(DEPTH, NA_HEADS, P, NT * T))

    def each(name, widths, group):
        return np.stack([_packed(w, widths, group) for w in a[name]])
    d["w_in"] = each("w_in", Z_WIDTHS, KD)
    d["w_uq"] = each("mla_w_uq", [384], 2)
    d["w_ukv"] = each("mla_w_ukv", [512], 1)
    d["w_pa"] = each("w_proj_a", [512] * 2, 2)
    d["w_pb"] = each("w_proj_b", [1024], 4)
    d["w_pc"] = each("w_proj_c", [1024], 2)
    d["w_out"] = each("w_out", [512] * 2, KD)
    d["mem_wq"] = each("mem_wq", [512] * 2, KD)
    d["mem_wkv"] = each("mem_wkv", [512] * 4, KD)
    d["mem_wo"] = each("mem_wo", [512] * 2, KD)
    d["ffn_up"], d["ffn_down"] = _experts(a["ffn_w_gu"], a["ffn_w_down"])
    d["moe_up"], d["moe_down"] = _experts(a["moe_w_gu"][0], a["moe_w_down"][0])
    d["router"] = a["moe_router"][0].reshape(KD, P, N_EXPERTS).transpose(1, 0, 2).reshape(P, -1)
    d["even_in"] = _packed(a["even_w_in_2"][0], [512] * 10, KD)
    d["even_out_att"] = _packed(a["even_w_out_2"][0][:D], [512] * 2, KD)
    d["even_out_ssm"] = _packed(a["even_w_out_2"][0][D:], [512] * 2, 4)
    d["glu"] = _packed(a["ssm_glu_w_2"][0], [512], 4)
    d["odd_in"] = _packed(a["odd_w_in_2"][0], [512] * 8, KD)
    d["odd_out"] = _packed(a["odd_w_out_2"][0], [512] * 2, 8)
    d["pool_w"] = np.stack([_packed(w, [512], 4) for w in a["pool_w_2"][0]])
    par = [a["ssm_a_re_2"][0], a["ssm_a_im_2"][0], np.repeat(a["ssm_log_dt_2"][0][:, None], 64, axis=1)]
    d["ssm_par"] = np.stack([p.reshape(SSM_TILES, P)[TILE_AT].T for p in par], axis=1).reshape(P, -1)
    w = np.zeros((P, 2, 1024), f)
    for c, (bm, cm) in enumerate(((a["ssm_b_re_2"][0], a["ssm_c_re_2"][0]), (a["ssm_b_im_2"][0], a["ssm_c_im_2"][0]))):
        vb = w[:, 0].reshape(P, 2, 4, P)
        vc = w[:, 1].reshape(P, 2, SSM_TILES, 32)
        for g in range(32):
            j, half = g // 2, g % 2
            q0 = 32 * (j % 4) + 16 * half
            vb[q0:q0 + 16, c, j // 4, 64 * half:64 * half + 64] = bm[g].T
            vc[64 * half:64 * half + 64, c, TILE_AT.index(j), 16 * half:16 * half + 16] = cm[g].T
    d["ssm_w"] = w.reshape(P, -1)
    d["ssm_vec"] = np.concatenate([a["ssm_d_2"][0], a["ssm_glu_b_2"][0]])[None]
    d["pool_scale"] = a["pool_scale_2"]
    return {k: np.ascontiguousarray(v) for k, v in d.items()}


def kernel(**inputs):
    import concourse.bacc as bacc
    from concourse.bass_utils import run_bass_kernel_spmd
    arrays = _layout(inputs)
    nc = bacc.Bacc("TRN2", target_bir_lowering=False, num_devices=1)
    d = {k: nc.dram_tensor(f"in_{k}", v.shape, F32, kind="ExternalInput").ap() for k, v in arrays.items()}
    out = nc.dram_tensor("out", (1, T, D), F32, kind="ExternalOutput").ap()
    program(nc, d, out)
    r = run_bass_kernel_spmd(nc, [{f"in_{k}": v for k, v in arrays.items()}], core_ids=[0])
    return r.results[0]["out"]
```
